# Optimizing a Trainium2 kernel written in Bass

```python
import math
import jax, jax.numpy as jnp
from jax import lax
import numpy as np

D_MODEL = 1024
BATCH = 1
SEQ = 128
DEPTH = 2
DEC_BATCH = 1
DEC_SEQ = 256
PAST_LEN = 128

GRID_W = 64
Q_BLOCK = 128
ROPE_BASE = 10000.0
EPS = 1e-6
N_EVEN = (DEPTH + 1) // 2
N_ODD = DEPTH // 2

CONV_CH = D_MODEL // 2
CONV_WIDTH = 31
CONV_PAD = CONV_WIDTH // 2
MLA_HEADS = 8
MLA_NOPE = 64
MLA_ROPE = 32
MLA_QK = MLA_NOPE + MLA_ROPE
MLA_V = 64
MLA_Q_RANK = 384
MLA_KV_RANK = 256
EVEN_IN = 2 * CONV_CH + MLA_Q_RANK + MLA_KV_RANK + MLA_ROPE
EVEN_OUT = CONV_CH + MLA_HEADS * MLA_V
DIFF_HEADS = 8
DIFF_DK = 64
DIFF_DV = 2 * DIFF_DK
DIFF_OUT = DIFF_HEADS * DIFF_DV
N_GROUPS = 4
EXPERTS_PER_GROUP = 8
N_EXPERTS = N_GROUPS * EXPERTS_PER_GROUP
TOP_K_IN_GROUP = 2
EXPERT_FF = 256

kernel_name = "hybrid_diffusion_conv_mla_diffattn_hmoe_step"

def rms_norm(x, g):
    xf = x.astype(jnp.float32)
    y = xf * lax.rsqrt(jnp.mean(xf * xf, axis=-1, keepdims=True) + EPS)
    return (y * g.astype(jnp.float32)).astype(x.dtype)

def layer_norm(x, g, b):
    xf = x.astype(jnp.float32)
    mu = jnp.mean(xf, axis=-1, keepdims=True)
    var = jnp.mean(jnp.square(xf - mu), axis=-1, keepdims=True)
    y = (xf - mu) * lax.rsqrt(var + EPS)
    return (y * g.astype(jnp.float32) + b.astype(jnp.float32)).astype(x.dtype)

def axial_rope_tables(n_tok, rot_dim):
    rows = n_tok // GRID_W
    row_ids = jnp.repeat(jnp.arange(rows, dtype=jnp.float32), GRID_W)
    col_ids = jnp.tile(jnp.arange(GRID_W, dtype=jnp.float32), rows)
    quarter = rot_dim // 4
    freqs = jnp.power(ROPE_BASE, -jnp.arange(quarter, dtype=jnp.float32) / quarter)
    ang = jnp.concatenate([row_ids[:, None] * freqs, col_ids[:, None] * freqs], axis=-1)
    return jnp.cos(ang), jnp.sin(ang)

def apply_rope(x, cos, sin):
    half = x.shape[-1] // 2
    shp = (cos.shape[0],) + (1,) * (x.ndim - 3) + (half,)
    c = cos.reshape(shp).astype(x.dtype)
    s = sin.reshape(shp).astype(x.dtype)
    x1, x2 = x[..., :half], x[..., half:]
    return jnp.concatenate([x1 * c - x2 * s, x1 * s + x2 * c], axis=-1)

def attend(q, k, v, scale):
    b, s = q.shape[0], q.shape[1]
    nb = s // Q_BLOCK
    qb = q.reshape((b, nb, Q_BLOCK) + q.shape[2:]).swapaxes(0, 1)

    def block(qi):
        sc = jnp.einsum('bqhmd,bkhmd->bhmqk', qi, k).astype(jnp.float32) * scale
        p = jax.nn.softmax(sc, axis=-1).astype(v.dtype)
        return jnp.einsum('bhmqk,bkhd->bqhmd', p, v)

    o = lax.map(block, qb)
    return o.swapaxes(0, 1).reshape((b, s) + o.shape[3:])

def conformer_conv(glu_in, w_dw, b_dw, ln_g, ln_b):
    a, gte = jnp.split(glu_in, 2, axis=-1)
    u = a * jax.nn.sigmoid(gte)
    y = lax.conv_general_dilated(u, w_dw[:, None, :].astype(u.dtype), window_strides=(1,),
                                 padding=[(CONV_PAD, CONV_PAD)],
                                 dimension_numbers=('NWC', 'WIO', 'NWC'),
                                 feature_group_count=CONV_CH) + b_dw
    return jax.nn.silu(layer_norm(y, ln_g, ln_b))

def mla_keys(c_kv, k_rope, w_kvb, kn_g):
    b, t = c_kv.shape[0], c_kv.shape[1]
    kv = (c_kv @ w_kvb).reshape(b, t, MLA_HEADS, MLA_NOPE + MLA_V)
    k_nope, v = kv[..., :MLA_NOPE], kv[..., MLA_NOPE:]
    k_r = jnp.broadcast_to(k_rope[:, :, None, :], (b, t, MLA_HEADS, MLA_ROPE))
    k = rms_norm(jnp.concatenate([k_nope, k_r], axis=-1), kn_g)
    return k, v

def even_mixer(h, P, e, ctx):
    b, s, _ = h.shape
    proj = h @ P['ev_w_in'][e]
    o1 = 2 * CONV_CH
    o2 = o1 + MLA_Q_RANK
    o3 = o2 + MLA_KV_RANK
    glu_in, q_a, kv_a, k_rope = proj[..., :o1], proj[..., o1:o2], proj[..., o2:o3], proj[..., o3:]
    conv_out = conformer_conv(glu_in, P['ev_conv_w'][e], P['ev_conv_b'][e],
                              P['ev_conv_ln_g'][e], P['ev_conv_ln_b'][e])
    q = (rms_norm(q_a, P['ev_q_norm_g'][e]) @ P['ev_w_qb'][e]).reshape(b, s, MLA_HEADS, MLA_QK)
    q = rms_norm(q, P['ev_qn_g'][e])
    c_kv = rms_norm(kv_a, P['ev_kv_norm_g'][e])
    k, v = mla_keys(c_kv, k_rope, P['ev_w_kvb'][e], P['ev_kn_g'][e])
    if ctx is not None:
        cos, sin = axial_rope_tables(s, MLA_ROPE)
        q = jnp.concatenate([q[..., :MLA_NOPE], apply_rope(q[..., MLA_NOPE:], cos, sin)], axis=-1)
        k = jnp.concatenate([k[..., :MLA_NOPE], apply_rope(k[..., MLA_NOPE:], cos, sin)], axis=-1)
        k_c, v_c = mla_keys(ctx[0], ctx[1], P['ev_w_kvb'][e], P['ev_kn_g'][e])
        k = jnp.concatenate([k, k_c], axis=1)
        v = jnp.concatenate([v, v_c], axis=1)
    o = attend(q[:, :, :, None, :], k[:, :, :, None, :], v, MLA_QK ** -0.5)[:, :, :, 0, :]
    out = jnp.concatenate([conv_out, o.reshape(b, s, MLA_HEADS * MLA_V)], axis=-1) @ P['ev_w_o'][e]
    return out, (c_kv, k_rope)

def diff_mixer(h, P, o_idx, lambda_init, ctx):
    b, s, _ = h.shape
    qkv = h @ P['od_w_qkv'][o_idx]
    q, k, v = jnp.split(qkv, 3, axis=-1)
    q = rms_norm(q.reshape(b, s, DIFF_HEADS, 2, DIFF_DK), P['od_qn_g'][o_idx])
    k = rms_norm(k.reshape(b, s, DIFF_HEADS, 2, DIFF_DK), P['od_kn_g'][o_idx])
    v = v.reshape(b, s, DIFF_HEADS, DIFF_DV)
    cache = (k, v)
    if ctx is not None:
        cos, sin = axial_rope_tables(s, DIFF_DK)
        q = apply_rope(q, cos, sin)
        k = jnp.concatenate([apply_rope(k, cos, sin), ctx[0]], axis=1)
        v = jnp.concatenate([v, ctx[1]], axis=1)
    o = attend(q, k, v, DIFF_DK ** -0.5)
    f32 = jnp.float32
    lam = (jnp.exp(jnp.sum(P['od_lambda_q1'][o_idx].astype(f32) * P['od_lambda_k1'][o_idx].astype(f32)))
           - jnp.exp(jnp.sum(P['od_lambda_q2'][o_idx].astype(f32) * P['od_lambda_k2'][o_idx].astype(f32)))
           + lambda_init)
    o = o[..., 0, :] - lam.astype(o.dtype) * o[..., 1, :]
    o = rms_norm(o, P['od_subln_g'][o_idx]) * (1.0 - lambda_init)
    return o.reshape(b, s, DIFF_OUT) @ P['od_w_o'][o_idx], cache

def hier_moe(h, P, l):
    b, s, d = h.shape
    t = h.reshape(-1, d)
    f32 = jnp.float32
    grp_prob = jax.nn.softmax((t @ P['moe_wg'][l]).astype(f32) + P['moe_bg'][l].astype(f32), axis=-1)
    grp_gate, grp_idx = lax.top_k(grp_prob, 1)
    exp_logits = ((t @ P['moe_we'][l]).astype(f32) + P['moe_be'][l].astype(f32)).reshape(-1, N_GROUPS, EXPERTS_PER_GROUP)
    sel = jnp.take_along_axis(exp_logits, grp_idx[:, :, None], axis=1)[:, 0, :]
    top_p, top_i = lax.top_k(jax.nn.softmax(sel, axis=-1), TOP_K_IN_GROUP)
    w = grp_gate * top_p / jnp.sum(top_p, axis=-1, keepdims=True)
    expert_ids = grp_idx * EXPERTS_PER_GROUP + top_i
    combine = jnp.sum(jax.nn.one_hot(expert_ids, N_EXPERTS, dtype=f32) * w[..., None], axis=1)

    def body(acc, xs):
        wg_e, wu_e, wd_e, cw = xs
        y = (jax.nn.silu(t @ wg_e) * (t @ wu_e)) @ wd_e
        return acc + cw[:, None].astype(t.dtype) * y, None

    acc, _ = lax.scan(body, jnp.zeros_like(t),
                      (P['moe_w_gate'][l], P['moe_w_up'][l], P['moe_w_down'][l], combine.T))
    return acc.reshape(b, s, d)

def trunk(x, cond, caches, P):
    mla_states, diff_states = [], []
    for l in range(DEPTH):
        mod = (jax.nn.silu(cond) @ P['ada_w'][l] + P['ada_b'][l])[:, None, :]
        sh1, sc1, g1, sh2, sc2, g2 = jnp.split(mod, 6, axis=-1)
        h = rms_norm(x, P['norm1_g'][l]) * (1 + sc1) + sh1
        if l % 2 == 0:
            e = l // 2
            ctx = None if caches is None else (caches[0][:, e], caches[1][:, e])
            out, st = even_mixer(h, P, e, ctx)
            mla_states.append(st)
        else:
            o_idx = l // 2
            ctx = None if caches is None else (caches[2][:, o_idx], caches[3][:, o_idx])
            lambda_init = 0.8 - 0.6 * math.exp(-0.3 * l)
            out, st = diff_mixer(h, P, o_idx, lambda_init, ctx)
            diff_states.append(st)
        x = x + g1 * out
        h = rms_norm(x, P['norm2_g'][l]) * (1 + sc2) + sh2
        x = x + g2 * hier_moe(h, P, l)
    return x, mla_states, diff_states

def setup_inputs(seed: int = 0) -> dict:
    key = jax.random.key(seed)
    ks = iter(jax.random.split(key, 64))
    f32 = jnp.float32

    def nrm(shape, scale=1.0):
        return jax.random.normal(next(ks), shape, f32) * scale

    def gain(shape):
        return 1.0 + nrm(shape, 0.02)

    D = D_MODEL
    return {
        'x_prompt': nrm((BATCH, SEQ, D)),
        'x_sample': nrm((DEC_BATCH, DEC_SEQ, D)),
        'cache_mla_ckv': nrm((DEC_BATCH, N_EVEN, PAST_LEN, MLA_KV_RANK)),
        'cache_mla_krope': nrm((DEC_BATCH, N_EVEN, PAST_LEN, MLA_ROPE)),
        'cache_diff_k': nrm((DEC_BATCH, N_ODD, PAST_LEN, DIFF_HEADS, 2, DIFF_DK)),
        'cache_diff_v': nrm((DEC_BATCH, N_ODD, PAST_LEN, DIFF_HEADS, DIFF_DV)),
        'c': nrm((DEC_BATCH, D)),
        'c_ctx': nrm((D,)),
        'ada_w': nrm((DEPTH, D, 6 * D), 0.5 * D ** -0.5),
        'ada_b': nrm((DEPTH, 6 * D), 0.02),
        'norm1_g': gain((DEPTH, D)),
        'norm2_g': gain((DEPTH, D)),
        'ev_w_in': nrm((N_EVEN, D, EVEN_IN), D ** -0.5),
        'ev_conv_w': nrm((N_EVEN, CONV_WIDTH, CONV_CH), CONV_WIDTH ** -0.5),
        'ev_conv_b': nrm((N_EVEN, CONV_CH), 0.02),
        'ev_conv_ln_g': gain((N_EVEN, CONV_CH)),
        'ev_conv_ln_b': nrm((N_EVEN, CONV_CH), 0.02),
        'ev_q_norm_g': gain((N_EVEN, MLA_Q_RANK)),
        'ev_w_qb': nrm((N_EVEN, MLA_Q_RANK, MLA_HEADS * MLA_QK), MLA_Q_RANK ** -0.5),
        'ev_kv_norm_g': gain((N_EVEN, MLA_KV_RANK)),
        'ev_w_kvb': nrm((N_EVEN, MLA_KV_RANK, MLA_HEADS * (MLA_NOPE + MLA_V)), MLA_KV_RANK ** -0.5),
        'ev_qn_g': gain((N_EVEN, MLA_QK)),
        'ev_kn_g': gain((N_EVEN, MLA_QK)),
        'ev_w_o': nrm((N_EVEN, EVEN_OUT, D), EVEN_OUT ** -0.5),
        'od_w_qkv': nrm((N_ODD, D, 3 * DIFF_OUT), D ** -0.5),
        'od_qn_g': gain((N_ODD, DIFF_DK)),
        'od_kn_g': gain((N_ODD, DIFF_DK)),
        'od_lambda_q1': nrm((N_ODD, DIFF_DK), 0.1),
        'od_lambda_k1': nrm((N_ODD, DIFF_DK), 0.1),
        'od_lambda_q2': nrm((N_ODD, DIFF_DK), 0.1),
        'od_lambda_k2': nrm((N_ODD, DIFF_DK), 0.1),
        'od_subln_g': gain((N_ODD, DIFF_DV)),
        'od_w_o': nrm((N_ODD, DIFF_OUT, D), DIFF_OUT ** -0.5),
        'moe_wg': nrm((DEPTH, D, N_GROUPS), D ** -0.5),
        'moe_bg': nrm((DEPTH, N_GROUPS), 0.01),
        'moe_we': nrm((DEPTH, D, N_EXPERTS), D ** -0.5),
        'moe_be': nrm((DEPTH, N_EXPERTS), 0.01),
        'moe_w_gate': nrm((DEPTH, N_EXPERTS, D, EXPERT_FF), D ** -0.5),
        'moe_w_up': nrm((DEPTH, N_EXPERTS, D, EXPERT_FF), D ** -0.5),
        'moe_w_down': nrm((DEPTH, N_EXPERTS, EXPERT_FF, D), EXPERT_FF ** -0.5),
    }

def reference(x_prompt, x_sample, cache_mla_ckv, cache_mla_krope, cache_diff_k, cache_diff_v, c, c_ctx,
              ada_w, ada_b, norm1_g, norm2_g,
              ev_w_in, ev_conv_w, ev_conv_b, ev_conv_ln_g, ev_conv_ln_b, ev_q_norm_g, ev_w_qb,
              ev_kv_norm_g, ev_w_kvb, ev_qn_g, ev_kn_g, ev_w_o,
              od_w_qkv, od_qn_g, od_kn_g, od_lambda_q1, od_lambda_k1, od_lambda_q2, od_lambda_k2,
              od_subln_g, od_w_o,
              moe_wg, moe_bg, moe_we, moe_be, moe_w_gate, moe_w_up, moe_w_down):
    P = dict(ada_w=ada_w, ada_b=ada_b, norm1_g=norm1_g, norm2_g=norm2_g,
             ev_w_in=ev_w_in, ev_conv_w=ev_conv_w, ev_conv_b=ev_conv_b, ev_conv_ln_g=ev_conv_ln_g,
             ev_conv_ln_b=ev_conv_ln_b, ev_q_norm_g=ev_q_norm_g, ev_w_qb=ev_w_qb,
             ev_kv_norm_g=ev_kv_norm_g, ev_w_kvb=ev_w_kvb, ev_qn_g=ev_qn_g, ev_kn_g=ev_kn_g, ev_w_o=ev_w_o,
             od_w_qkv=od_w_qkv, od_qn_g=od_qn_g, od_kn_g=od_kn_g, od_lambda_q1=od_lambda_q1,
             od_lambda_k1=od_lambda_k1, od_lambda_q2=od_lambda_q2, od_lambda_k2=od_lambda_k2,
             od_subln_g=od_subln_g, od_w_o=od_w_o,
             moe_wg=moe_wg, moe_bg=moe_bg, moe_we=moe_we, moe_be=moe_be,
             moe_w_gate=moe_w_gate, moe_w_up=moe_w_up, moe_w_down=moe_w_down)
    y_prompt, mla_states, diff_states = trunk(x_prompt, c_ctx[None, :], None, P)
    y_sample, _, _ = trunk(x_sample, c, (cache_mla_ckv, cache_mla_krope, cache_diff_k, cache_diff_v), P)
    new_mla_ckv = jnp.stack([st[0] for st in mla_states], axis=1)
    new_mla_krope = jnp.stack([st[1] for st in mla_states], axis=1)
    new_diff_k = jnp.stack([st[0] for st in diff_states], axis=1)
    new_diff_v = jnp.stack([st[1] for st in diff_states], axis=1)
    return (y_prompt, y_sample, new_mla_ckv, new_mla_krope, new_diff_k, new_diff_v)


_drawn_inputs = setup_inputs


def setup_inputs(seed=0):
    import zlib

    import numpy as np

    out = dict(_drawn_inputs(seed))
    spreads = {}
    factors = {'cache_mla_ckv': 4.272,
     'cache_mla_krope': 5.869,
     'norm1_g': 2.919,
     'norm2_g': 3.409,
     'ev_conv_b': 8.0,
     'ev_conv_ln_g': 8.0,
     'ev_conv_ln_b': 8.0,
     'ev_q_norm_g': 8.0,
     'ev_kv_norm_g': 2.889,
     'ev_qn_g': 8.0,
     'ev_kn_g': 8.0,
     'od_qn_g': 8.0,
     'od_kn_g': 3.174,
     'od_lambda_k2': 8.0,
     'od_subln_g': 8.0,
     'moe_bg': 8.0,
     'moe_be': 7.704,
     'cache_diff_k': 8.0,
     'cache_diff_v': 8.0}
    for name, (base, spread) in spreads.items():
        noise = np.random.default_rng([zlib.crc32(name.encode()), seed]).standard_normal(out[name].shape)
        drawn = base * np.exp(spread * noise) if base else spread * noise
        out[name] = __import__('jax').numpy.asarray(drawn.astype(out[name].dtype))
    for name, factor in factors.items():
        out[name] = (out[name] * factor).astype(out[name].dtype)
    return out
```

```python
import math
from contextlib import ExitStack

import numpy as np

import concourse.bass as bass
from concourse import mybir

ALU = mybir.AluOpType
ACT = mybir.ActivationFunctionType
AX = mybir.AxisListType
F32 = mybir.dt.float32
U32 = mybir.dt.uint32
I32 = mybir.dt.int32

P = 128
D = 1024
KD = D // P
DEPTH = 2
CTX, LAT = 128, 256
TOK = CTX + LAT
NT = TOK // P
PAST = 128
EPS = 1e-6
CH, TAPS = 512, 31
NCH, PADC = CH // P, TAPS // 2
QR, KVR, ROPE, NOPE, HEADS = 384, 256, 32, 64, 8
QK = NOPE + ROPE
EVEN_IN = 2 * CH + QR + KVR + ROPE
REST = QR + KVR + ROPE
DK, DV = 64, 128
NG, EPG, NE, FF = 4, 8, 32, 256
ROWS = 64
ROUNDS = TOK // ROWS
PAIRS = 2 * TOK
RING = 6
BUFFERS = 2
UNROLL = 4
STEPS_AHEAD = 4
BODIES = (NE - 1 - STEPS_AHEAD) // UNROLL
PAIR_ROUNDS = KD // 2
SLOT = 2048
CONVW = PADC + CTX + PADC + LAT + PADC
CONVO = CTX + PADC + LAT
LAMBDA_INIT = 0.8 - 0.6 * math.exp(-0.3)
BIG = 1e30
SEG = ((0, CTX, 0), (CTX, TOK, 1))

B_QN, B_KN, B_DQN, B_DKN = 0, 96, 192, 256
B_SUB, B_KVN, B_LAM, B_MOE = 320, 448, 704, 960
NBC = B_MOE + DEPTH * (NG + NE)
M_WORK, M_EQ, M_SEL, M_SEL2, M_ONE1, M_ONE2, M_BOTH, M_PLACE, M_RANK = range(9)
(R_GMAX, R_GSUM, R_GATE, R_GTOP, R_M1, R_TOP1, R_M2, R_TOP2, R_D, R_ED, R_RANK1, R_RANK2, R_ID1, R_ID2,
 R_W1, R_W2, R_P1, R_P2, R_TURN) = range(19)
C_ADA, C_N1, C_N2 = 0, 96, 112
C_CW, C_CB = 128, 252
C_LNG, C_LNB, C_QRG, C_COND, C_CCTX = 256, 260, 264, 267, 275
NCOL = 283

MATERIAL = ["x_prompt", "x_sample", "cache_mla_ckv", "cache_mla_krope", "cache_diff_k", "cache_diff_v",
            "c", "c_ctx", "ada_w", "ada_b", "norm1_g", "norm2_g", "ev_w_in", "ev_conv_w", "ev_conv_b",
            "ev_conv_ln_g", "ev_conv_ln_b", "ev_q_norm_g", "ev_w_qb", "ev_kv_norm_g", "ev_w_kvb",
            "ev_qn_g", "ev_kn_g", "ev_w_o", "od_w_qkv", "od_qn_g", "od_kn_g", "od_lambda_q1",
            "od_lambda_k1", "od_lambda_q2", "od_lambda_k2", "od_subln_g", "od_w_o", "moe_wg", "moe_bg",
            "moe_we", "moe_be", "moe_w_gate", "moe_w_up", "moe_w_down"]


class PsumGroups:

    def __init__(self, start=0):
        self.names, self.at, self.reader, self.count = [], {}, [], []
        self.read = {"v": 0, "s": 0}

    def add(self, name, reader):
        self.at[name] = len(self.names)
        self.names.append(name)
        self.reader.append(reader)
        self.read[reader] += 1
        self.count.append(self.read[reader])


def attention_units(l):
    return [(h, t, m) for h in range(HEADS) for t in range(NT) for m in range((1, 2)[l])]


IN_BLOCKS = [("glu_a", (0, 1)), ("glu_g", (0, 1)), ("glu_a", (2, 3)), ("glu_g", (2, 3)), ("rest", 0), ("rest", 1), ("rest", 2)]
ADA_AFTER_BLOCK = {1: (0, 2), 2: (0, 3), 3: (0, 4), 4: (0, 5), 5: (1, 0)}
ADA_AT_STEP = {2 + 5 * i: (1, 1 + i) for i in range(5)}
ADA_LAG = 3


def attention_steps(l):
    n = len(attention_units(l))
    width, lag = ((1, 2), (2, 1))[l]
    for s in range(n // width + lag + 1):
        def units(behind):
            return [u for u in range(width * (s - behind), width * (s - behind) + width) if 0 <= u < n]
        yield (units(0), units(lag), units(lag + 1),
               ADA_AT_STEP.get(s) if l == 0 else None, ADA_AT_STEP.get(s - ADA_LAG) if l == 0 else None)


def psum_order():
    g = PsumGroups()
    g.add("vectors", "v")
    for c in range(KD):
        g.add(("xT", c), "s")
    g.add(("sumsq", 0, 0), "s")
    for s in range(2):
        g.add(("ada", 0, s), "s")
        g.add(("adaT", 0, s), "v")
    for l in range(DEPTH):
        if l == 0:
            for i, (kind, js) in enumerate(IN_BLOCKS):
                if kind == "rest":
                    for t in range(NT):
                        g.add(("rest", js, t), "s")
                else:
                    for j in js:
                        g.add((kind, j), "s")
                if i - 1 in ADA_AFTER_BLOCK:
                    g.add(("adaT",) + ADA_AFTER_BLOCK[i - 1], "v")
                if i in ADA_AFTER_BLOCK:
                    g.add(("ada",) + ADA_AFTER_BLOCK[i], "s")
            for j in range(3):
                g.add(("qanT", j), "s")
            for j in range(2):
                g.add(("ckvT", j), "v")
            for b in range(2):
                for t in range(NT):
                    g.add(("q", b, t), "v")
            for t in range(NT + 1):
                for b in range(2):
                    g.add(("kv", t, b), "s")
        else:
            g.add(("sumsq", l, 0), "s")
            for b in range(12):
                for t in range(NT):
                    g.add(("qkv", b, t), "sv"[(b * NT + t) % 2])
        for h in range(HEADS):
            g.add(("qT", l, h), "s")
        for h in range(HEADS):
            g.add(("kT", l, h), "v")
        for scores, turned, outs, sums, columns in attention_steps(l):
            for u in scores:
                g.add(("S", l, u), "s")
            for u in turned:
                g.add(("pT", l, u), "s")
            for u in outs:
                g.add(("o", l, u), "v")
            if sums:
                g.add(("ada",) + sums, "s")
            if columns:
                g.add(("adaT",) + columns, "v")
        for j in range((NCH, KD)[l]):
            g.add(("oT", l, j), "s")
        if l == 0:
            g.add("conv_mean", "v")
            g.add("conv_var", "s")
        for c in range(KD):
            g.add(("out", l, c), "v")
        g.add(("sumsq", l, 1), "s")
        g.add(("router", l), "v")
        for t in range(NT):
            for b in range(2):
                g.add(("htok", l, t, b), "s")
        g.add(("rank", l), "v")
        for i in range(NT):
            g.add(("codes", l, i), "s")
    for t in range(NT):
        for b in range(2):
            g.add(("final", t, b), "sv"[b])
    return g


def weight_order():
    out = []

    def ada(l, s):
        for k in range(4):
            out.append((("ada", l, s, k), ("ada", l, s)))

    for l in range(DEPTH):
        if l == 0:
            ada(0, 0)
            ada(0, 1)
            for i, (kind, js) in enumerate(IN_BLOCKS):
                if kind == "rest":
                    out.append((("w_in", 4 + js), ("rest", js, 2)))
                else:
                    out.append((("w_in", js[0] // 2 + (0 if kind == "glu_a" else 2)), (kind, js[1])))
                if i in ADA_AFTER_BLOCK:
                    ada(*ADA_AFTER_BLOCK[i])
            for b in range(2):
                out.append((("w_qb", b), ("q", b, 2)))
            out.append((("w_kvb",), ("kv", 3, 1)))
            for s in sorted(ADA_AT_STEP):
                ada(*ADA_AT_STEP[s])
        else:
            for b in range(12):
                out.append((("w_qkv", b), ("qkv", b, 2)))
        for b in range(4):
            out.append((("w_o", l, b), ("out", l, 2 * b + 1)))
        out.append(("experts", l))
    return out


def hybrid_trunk(nc, ins, tables, outs):
    (x_prompt, x_sample, c_ckv, c_krope, c_dk, c_dv, c_vec, c_ctx, ada_w, ada_b, n1g, n2g, w_in, conv_w,
     conv_b, ln_g, ln_b, qr_g, w_qb, kvn_g, w_kvb, qn_g, kn_g, ev_wo, w_qkv, dqn_g, dkn_g, lq1, lk1, lq2,
     lk2, sub_g, od_wo, moe_wg, moe_bg, moe_we, moe_be, e_gate, e_up, e_down) = ins
    rope_mla, rope_diff = tables
    y_prompt, y_sample, new_ckv, new_krope, new_dk, new_dv = outs
    groups = psum_order()
    sorted_rows = nc.dram_tensor("sorted_rows", (PAIRS + ROWS, D), F32, kind="Internal").ap()

    with ExitStack() as ctx:
        def sb(name, shape, dt=F32):
            return ctx.enter_context(nc.sbuf_tensor(name, shape, dt))

        sems = {}

        def sem(name):
            if name not in sems:
                sems[name] = ctx.enter_context(nc.semaphore(name))
            return sems[name]

        banks = ctx.enter_context(nc.psum_tensor("banks", [P, 8, 512], F32))
        bank = [banks[:, i, :] for i in range(8)]

        ring = sb("ring", [P, RING, SLOT])
        xT = sb("xT", [P, KD, TOK])
        hT = sb("hT", [P, KD, TOK])
        a1 = sb("a1", [P, 3072])
        a2 = sb("a2", [P, 4096])
        a3 = sb("a3", [P, 4096])
        a4 = sb("a4", [P, 3072])
        a5 = sb("a5", [P, 4096])
        a6 = sb("a6", [P, 3072])
        a7 = sb("a7", [P, 1536 + NCH * CONVW])
        wr = sb("wr", [P, DEPTH, KD, NG + NE])
        cols = sb("cols", [P, NCOL])
        bc = sb("bc", [P, NBC])
        mod = sb("mod", [P, DEPTH, 6, KD, 2])
        condS = sb("condS", [P, KD, 32])
        ada_rows = sb("ada_rows", [P, 512])
        pick = sb("pick", [P, 2, 2])
        ident = sb("ident", [P, P])
        ones = sb("ones", [P, P])
        below = sb("below", [P, P])
        ramp = sb("ramp", [P, NE])
        turn_row = sb("turn_row", [P, NE])
        rope16 = sb("rope16", [P, 2, 2, ROPE // 2])
        rope32 = sb("rope32", [P, 2, 2, DK // 2])
        eps = sb("eps", [P, 1])
        iota = sb("iota", [P, NE], I32)
        std = sb("std", [P, CONVO])
        rstd = sb("rstd", [P, CONVO])
        pbuf = sb("pbuf", [P, 4, TOK])
        pTbuf = sb("pTbuf", [P, 4, 3, P])
        small = sb("small", [P, 8, 64])
        negmax = sb("negmax", [P, 48])
        rowsum = sb("rowsum", [P, 48])
        rinv = sb("rinv", [P, 48])
        lam = sb("lam", [P, 8])
        rt = sb("rt", [P, 10, NT * NE])
        rs = sb("rs", [P, 20, NT])
        logits = sb("logits", [P, NT, NG + NE])
        prefix = sb("prefix", [P, 2, 16 + NE])
        idx_sorted = sb("idx_sorted", [P, 2 * NT], U32)
        row_of = sb("row_of", [P, 1])
        row_iota = sb("row_iota", [P, 1], I32)
        further_code = sb("further_code", [P, 1])
        starts = sb("starts", [P, ROUNDS * NE], I32)
        overflow = sb("overflow", [P, DEPTH], I32)
        sgate = a6[0:ROWS, 0:BUFFERS * FF].rearrange("p (b f) -> p b f", b=BUFFERS)
        hid = a6[0:ROWS, BUFFERS * FF:2 * BUFFERS * FF].rearrange("p (b f) -> p b f", b=BUFFERS)
        hidT = a6[:, 2 * BUFFERS * FF:2 * BUFFERS * FF + 2 * BUFFERS * ROWS].rearrange("p (b j r) -> p b j r", b=BUFFERS, j=2)

        xtok = a1[:, :].rearrange("p (t d) -> p t d", t=NT)
        htok = xtok
        packs = a6[:, 0:3 * P].rearrange("p (a b) -> p a b", a=3)
        scratch = a6[:, :]
        hn = a6[:, :].rearrange("p (c t) -> p c t", c=KD)
        glu_a = a6[:, 0:NCH * TOK].rearrange("p (c t) -> p c t", c=NCH)
        glu_g = a6[:, NCH * TOK:2 * NCH * TOK].rearrange("p (c t) -> p c t", c=NCH)
        proj = a5[:, 0:NT * REST].rearrange("p (t n) -> p t n", t=NT)
        ckv = a5[:, NT * REST:NT * REST + 4 * KVR].rearrange("p (t n) -> p t n", t=4)
        krope_c = a5[:, NT * REST + 4 * KVR:NT * REST + 4 * KVR + ROPE]
        qanT = a4[:, 0:3 * TOK].rearrange("p (c t) -> p c t", c=3)
        ckvT = a4[:, 3 * TOK:3 * TOK + 2 * 512].rearrange("p (c t) -> p c t", c=2)
        q_e = a1[:, 0:NT * HEADS * QK].rearrange("p (t n) -> p t n", t=NT)
        k_e = a2[:, 0:4 * HEADS * QK].rearrange("p (t h e) -> p t h e", t=4, h=HEADS)
        v_e = a3[:, 0:4 * HEADS * NOPE].rearrange("p (t n) -> p t n", t=4)
        conv_acc = a3[:, 2048:2048 + NCH * CONVO].rearrange("p (c t) -> p c t", c=NCH)
        qT = a4[:, :].rearrange("p (h t) -> p h t", h=HEADS)
        kT = a5[:, :].rearrange("p (h t) -> p h t", h=HEADS)
        o_e = a7[:, 0:NT * CH].rearrange("p (t n) -> p t n", t=NT)
        uT = a7[:, NT * CH:NT * CH + NCH * CONVW].rearrange("p (c t) -> p c t", c=NCH)
        rope_tmp = a7[:, 0:3 * 512].rearrange("p (k n) -> p k n", k=3)
        q_o = a1[:, :].rearrange("p (t n) -> p t n", t=NT)
        k_o = a2[:, :].rearrange("p (t n) -> p t n", t=4)
        v_o = a3[:, :].rearrange("p (t n) -> p t n", t=4)
        o_o = a7[:, 0:NT * D].rearrange("p (t n) -> p t n", t=NT)
        te = [a4[0:ROWS, i * D:(i + 1) * D] for i in range(BUFFERS)]
        teT = [a5[:, i * 512:(i + 1) * 512].rearrange("p (c r) -> p c r", c=KD) for i in range(BUFFERS)]
        y_pair = [a5[:, D + i * D:2 * D + i * D] for i in range(BUFFERS)]
        y_further = a5[0:ROWS, 3 * D:4 * D]
        moe_sum = hT
        spread = a6[:, 2 * BUFFERS * FF + 2 * BUFFERS * ROWS:2 * BUFFERS * FF + 2 * BUFFERS * ROWS + 2 * TOK + BUFFERS * TOK]
        chosen_by = spread[:, 0:2 * TOK]
        weights_at = [spread[:, 2 * TOK + i * TOK:3 * TOK + i * TOK] for i in range(BUFFERS)]
        diagonals = a7[:, 0:4 * TOK].rearrange("p (a q) -> p a q", q=P)
        pair_codes = a7[:, 4 * TOK:4 * TOK + NE // 2]
        pair_rows = a7[:, 4 * TOK + NE:8 * TOK + NE]
        xout = a2[:, 0:3072].rearrange("p (t d) -> p t d", t=NT)
        conv_sq = a6[:, 0:NCH * CONVO].rearrange("p (c t) -> p c t", c=NCH)
        gsub, gexp, geq, grank, gone, gpen = (rt[:, 9, NT * NG * i:NT * NG * i + NT * NG] for i in range(6))

        order = weight_order()
        piece_at, waits_of, base_of = {}, [], {}
        n = 0
        for item in order:
            if item[0] == "experts":
                base_of[item[1]] = n
                n += 3 * NE
            else:
                piece_at[item[0]] = n
                n += 1
        last_reader = {piece_at[i[0]]: i[1] for i in order if i[0] != "experts"}

        def slot(i):
            return ring[:, i % RING, :]

        def landed(i, turns=0):
            return 16 * (i // RING + 1) + 16 * turns

        def slot_sem(i):
            return sem(f"slot{i % RING}_landed")

        def piece(kind, *key):
            return piece_at[(kind,) + key]

        def expert_piece(l, n, k):
            return base_of[l] + 3 * n + k

        def is_read(eng, name):
            i = groups.at[name]
            eng.wait_ge(sem({"v": "read_by_vector", "s": "read_by_scalar"}[groups.reader[i]]), groups.count[i])

        def is_filled(eng, name):
            eng.wait_ge(sem("filled"), groups.at[name] + 1)

        def psum(name):
            return bank[groups.at[name] % 8][:, :]

        def mcol(l, s, c, j):
            return mod[:, l, s, c, j:j + 1]

        def col(i):
            return cols[:, i:i + 1]

        def further_turns(eng, l, turn, until=None):
            eng.wait_ge(sem("starts_ready"), l + 1)
            many = eng.value_load(overflow[0:1, l:l + 1], min_val=0, max_val=1)
            with eng.If(many > 0):
                with eng.Fori(0, (ROUNDS - 1) * NE) as i:
                    turn(i)
                if until:
                    eng.wait_ge(sem(until[0]), until[1])

        def tile(t):
            return slice(P * t, P * t + P)

        block = ctx.enter_context(nc.Block())

        @block.sync
        def _(sp):
            sp.dma_start(packs[0:96, 0, :], ada_b.rearrange("l (n p) -> (l n) p", p=P)).then_inc(sem("vectors_loaded"), 16)
            sp.dma_start(packs[96:112, 0, :], n1g.rearrange("l (n p) -> (l n) p", p=P)).then_inc(sem("vectors_loaded"), 16)
            sp.dma_start(packs[112:128, 0, :], n2g.rearrange("l (n p) -> (l n) p", p=P)).then_inc(sem("vectors_loaded"), 16)
            at = 0
            for v in (ln_g[0], ln_b[0], qr_g[0], c_vec[0], c_ctx):
                k = v.shape[0] // P
                sp.dma_start(packs[at:at + k, 2, :], v.rearrange("(n p) -> n p", p=P)).then_inc(sem("vectors_loaded"), 16)
                at += k
            sp.dma_start(packs[0:124, 1, :], conv_w[0].rearrange("t (n p) -> (t n) p", p=P)).then_inc(sem("vectors_loaded"), 16)
            sp.dma_start(packs[124:128, 1, :], conv_b[0].rearrange("(n p) -> n p", p=P)).then_inc(sem("vectors_loaded"), 16)

            def load_piece(i, src, width):
                sp.dma_start(slot(i)[:, 0:width].rearrange("p (k n) -> p k n", k=src.shape[1]), src).then_inc(slot_sem(i), 16)

            def free(i):
                if i >= RING and i - RING in last_reader:
                    sp.wait_ge(sem("filled"), groups.at[last_reader[i - RING]] + 1)
                elif i >= RING:
                    sp.wait_ge(sem("down_filled"), NE)

            def source(name):
                if name[0] == "ada":
                    _, l, s, k = name
                    return ada_w[l, 256 * k:256 * k + 256, D * s:D * s + D].rearrange("(k p) n -> p k n", p=P)
                if name[0] == "w_in":
                    b = name[1]
                    return w_in[0, :, 256 * b:min(256 * b + 256, EVEN_IN)].rearrange("(k p) n -> p k n", p=P)
                if name[0] == "w_qb":
                    return w_qb[0, :, 384 * name[1]:384 * name[1] + 384].rearrange("(k p) n -> p k n", p=P)
                if name[0] == "w_kvb":
                    return w_kvb[0].rearrange("(k p) n -> p k n", p=P)
                if name[0] == "w_qkv":
                    return w_qkv[0, :, 256 * name[1]:256 * name[1] + 256].rearrange("(k p) n -> p k n", p=P)
                w = (ev_wo, od_wo)[name[1]]
                return w[0, :, 256 * name[2]:256 * name[2] + 256].rearrange("(k p) n -> p k n", p=P)

            def expert_loads(l):
                def weights(n, t, steady, which=(0, 1, 2)):
                    for k in which:
                        w, used = ((e_gate, "gate_up_filled"), (e_up, "gate_up_filled"), (e_down, "down_filled"))[k]
                        i = expert_piece(l, n, k)
                        if steady:
                            sp.wait_ge(sem(used), BUFFERS * t + (NE * l + n - 1))
                        else:
                            free(i)
                        e = bass.ds(BUFFERS * t + n, 1)
                        sp.dma_start(slot(i), w[l, e].rearrange("e (p k) n -> (e p) (k n)", p=P)).then_inc(slot_sem(i), 16)

                def token_rows(n, t, steady):
                    if steady or l:
                        sp.wait_ge(sem("rows_turned"), BUFFERS * t + (NE * l + n - 1))
                    first = sp.value_load(starts[0:1, bass.ds(BUFFERS * t + n, 1)], min_val=0, max_val=PAIRS)
                    sp.dma_start(te[n % BUFFERS], sorted_rows[bass.ds(first, ROWS), :]).then_inc(sem(f"rows{n % BUFFERS}_loaded"), 16)

                for n in range(BUFFERS):
                    weights(n, 0, False)
                sp.wait_ge(sem("rows_sorted"), 16 * 2 * NT * (l + 1))
                sp.wait_ge(sem("starts_ready"), l + 1)
                for n in range(BUFFERS):
                    token_rows(n, 0, False)
                for n in range(BUFFERS, BUFFERS + 1):
                    token_rows(n, 0, True)
                    weights(n, 0, True, (0, 1))
                token_rows(BUFFERS + 1, 0, True)
                with sp.Fori(0, (NE - 2 * BUFFERS) // BUFFERS) as t:
                    for n in range(BUFFERS + 1, 2 * BUFFERS + 1):
                        token_rows(n + 1, t, True)
                        weights(n, t, True, (0, 1))
                        weights(n - 1, t, True, (2,))
                weights(NE - 1, 0, True, (0, 1))
                weights(NE - 2, 0, True, (2,))
                weights(NE - 1, 0, True, (2,))

                def loads(j, e, i):
                    first = sp.value_load(starts[0:1, bass.ds(i + NE, 1)], min_val=0, max_val=PAIRS)
                    loaded = sem(f"further{l}_loaded")
                    if not (isinstance(i, int) and i == 0):
                        sp.wait_ge(sem(f"further{l}_added"), PAIR_ROUNDS * i)
                    sp.dma_start(te[0], sorted_rows[bass.ds(first, ROWS), :]).then_inc(loaded, 16)
                    for k, w in enumerate((e_gate, e_up, e_down)):
                        sp.dma_start(ring[:, k, :], w[l, bass.ds(e, 1)].rearrange("e (p k) n -> (e p) (k n)", p=P)).then_inc(loaded, 16)

                many = sp.value_load(overflow[0:1, l:l + 1], min_val=0, max_val=1)
                with sp.If(many > 0):
                    sp.wait_ge(sem("spread_added"), PAIR_ROUNDS * NE // 2 * (l + 1))
                    loads(0, 0, 0)
                    with sp.Fori(1, NE) as e:
                        loads(0, e, e)
                    with sp.Fori(1, ROUNDS - 1) as j:
                        with sp.Fori(0, NE) as e:
                            loads(j, e, NE * j + e)
                    sp.wait_ge(sem(f"further{l}_added"), PAIR_ROUNDS * (ROUNDS - 1) * NE)

            for item in order:
                if item[0] == "experts":
                    expert_loads(item[1])
                else:
                    i = piece_at[item[0]]
                    free(i)
                    if item[0] == ("w_in", 4):
                        sp.wait_ge(sem("filled"), groups.at[("xT", KD - 1)] + 1)
                        sp.dma_start(ckv[:, 3, :], c_ckv[0, 0]).then_inc(sem("cache_loaded"), 16)
                        sp.dma_start(krope_c, c_krope[0, 0]).then_inc(sem("cache_loaded"), 16)
                    if item[0] == ("w_qkv", 4):
                        sp.wait_ge(sem("filled"), groups.at[("out", 0, 0)] + 1)
                        sp.dma_start(k_o[:, 3, :], c_dk[0, 0].rearrange("p h m d -> p (h m d)")).then_inc(sem("cache_loaded"), 16)
                        sp.dma_start(v_o[:, 3, :], c_dv[0, 0].rearrange("p h d -> p (h d)")).then_inc(sem("cache_loaded"), 16)
                    src = source(item[0])
                    load_piece(i, src, src.shape[1] * src.shape[2])
            for t in range(NT):
                for b in range(2):
                    is_read(sp, ("final", t, b))
                dst = y_prompt[0] if t == 0 else y_sample[0, P * (t - 1):P * t, :]
                sp.dma_start(dst, xout[:, t, :]).then_inc(sem("y_stored"), 16)
            sp.wait_ge(sem("y_stored"), 16 * NT)

        @block.tensor
        def _(pe):
            at = [0]

            def opened(name):
                i = groups.at[name]
                assert i == at[0], (name, i, at[0])
                at[0] += 1
                if i >= 8:
                    is_read(pe, groups.names[i - 8])
                return psum(name)

            def product(out, pairs, last=False, ready=None):
                for k, (lhsT, rhs) in enumerate(pairs):
                    if ready:
                        ready(k)
                    mm = pe.matmul(out, lhsT, rhs, start=(k == 0), stop=(k == len(pairs) - 1))
                if last:
                    mm.then_inc(sem("filled"), 1)

            def turn(out, parts):
                column = 0
                for part in parts:
                    r, w = part.shape[0], part.shape[1]
                    mm = pe.transpose(out[0:w, column:column + r], part, ident[0:r, 0:r])
                    column += r
                mm.then_inc(sem("filled"), 1)

            def arrived(*name):
                i = piece_at[name]
                pe.wait_ge(slot_sem(i), landed(i))
                return slot(i)

            def chunk_of_h(use):
                def ready(k):
                    pe.wait_ge(sem("h_lat_ready"), KD * use + k + 1)
                    pe.wait_ge(sem("h_ctx_ready"), KD * use + k + 1)
                return ready

            def ada_sums(l, s):
                out = opened(("ada", l, s))
                for k in range(0, KD, 2):
                    w = arrived("ada", l, s, k // 2).rearrange("p (k n) -> p k n", k=2)
                    for odd in range(2):
                        for half in range(2):
                            q = 32 * (2 * odd + half)
                            mm = pe.matmul(out[q:q + 32, :], condS[:, k + odd, :], w[:, odd, 512 * half:512 * half + 512],
                                           start=(k == 0), stop=(k == KD - 2), tile_position=(0, q))
                mm.then_inc(sem("filled"), 1)

            def ada_columns(l, s):
                out = opened(("adaT", l, s))
                is_read(pe, ("ada", l, s))
                for n in range(KD):
                    mm = pe.matmul(out[:, 2 * n:2 * n + 2], ada_rows[:, P * (n % 4):P * (n % 4) + P], pick[:, n // 4, :],
                                   start=True, stop=True)
                mm.then_inc(sem("filled"), 1)

            def sum_of_squares(l, w):
                out = opened(("sumsq", l, w))
                for c in range(KD):
                    pe.wait_ge(sem("squares_ready"), KD * (2 * l + w) + c + 1)
                    mm = pe.matmul(out[:, 0:TOK], ones[:, :], scratch[:, c * TOK:c * TOK + TOK],
                                   start=(c == 0), stop=(c == KD - 1))
                mm.then_inc(sem("filled"), 1)

            def even_projections():
                for i, (kind, js) in enumerate(IN_BLOCKS):
                    if kind == "rest":
                        width = min(256, REST - 256 * js)
                        w = arrived("w_in", 4 + js)[:, 0:KD * width].rearrange("p (k n) -> p k n", k=KD)
                        for t in range(NT):
                            product(opened(("rest", js, t))[:, 0:width],
                                    [(hT[:, k, tile(t)], w[:, k, :]) for k in range(KD)], True)
                    else:
                        w = arrived("w_in", js[0] // 2 + (0 if kind == "glu_a" else 2)).rearrange("p (k n) -> p k n", k=KD)
                        for j in js:
                            product(opened((kind, j))[:, 0:TOK],
                                    [(w[:, k, P * (j % 2):P * (j % 2) + P], hT[:, k, :]) for k in range(KD)], True,
                                    chunk_of_h(0) if i == 0 and j == 0 else None)
                    if i - 1 in ADA_AFTER_BLOCK:
                        ada_columns(*ADA_AFTER_BLOCK[i - 1])
                    if i in ADA_AFTER_BLOCK:
                        ada_sums(*ADA_AFTER_BLOCK[i])
                pe.wait_ge(sem("qa_normed"), NT)
                for j in range(3):
                    turn(opened(("qanT", j)), [proj[:, t, P * j:P * j + P] for t in range(NT)])
                pe.wait_ge(sem("ckv_normed"), NT)
                pe.wait_ge(sem("cache_loaded"), 32)
                for j in range(2):
                    turn(opened(("ckvT", j)), [ckv[:, t, P * j:P * j + P] for t in range(4)])
                is_read(pe, ("qanT", 2))
                for b in range(2):
                    w = arrived("w_qb", b)[:, 0:3 * 384].rearrange("p (k n) -> p k n", k=3)
                    for t in range(NT):
                        product(opened(("q", b, t))[:, 0:384],
                                [(qanT[:, k, tile(t)], w[:, k, :]) for k in range(3)], True)
                is_read(pe, ("ckvT", 1))
                w = arrived("w_kvb").rearrange("p (k n) -> p k n", k=2)
                for t in range(NT + 1):
                    for b in range(2):
                        product(opened(("kv", t, b)), [(ckvT[:, k, tile(t)], w[:, k, 512 * b:512 * b + 512]) for k in range(2)], True)


            def odd_projections():
                for b in range(12):
                    w = arrived("w_qkv", b).rearrange("p (k n) -> p k n", k=KD)
                    for t in range(NT):
                        product(opened(("qkv", b, t))[:, 0:256],
                                [(hT[:, k, tile(t)], w[:, k, :]) for k in range(KD)], True,
                                chunk_of_h(2) if b == 0 and t == 0 else None)

            def turned_heads(l):
                pe.wait_ge(sem("q_ready"), l + 1)
                for h in range(HEADS):
                    src = q_e[:, :, QK * h:QK * h + QK] if l == 0 else q_o[:, :, P * h:P * h + P]
                    turn(opened(("qT", l, h)), [src[:, t, :] for t in range(NT)])
                pe.wait_ge(sem("k_ready"), l + 1)
                if l == 1:
                    pe.wait_ge(sem("cache_loaded"), 64)
                for h in range(HEADS):
                    src = k_e[:, :, h, :] if l == 0 else k_o[:, :, P * h:P * h + P]
                    turn(opened(("kT", l, h)), [src[:, t, :] for t in range(4)])

            def attention(l):
                units = attention_units(l)
                is_read(pe, ("qT", l, HEADS - 1))
                is_read(pe, ("kT", l, HEADS - 1))
                for scores, turned, outs, sums, columns in attention_steps(l):
                    for u in scores:
                        h, t, m = units[u]
                        out = opened(("S", l, u))
                        part = slice(0, QK) if l == 0 else slice(DK * m, DK * m + DK)
                        keys = slice(0, P) if t == 0 else slice(P, 4 * P)
                        n = keys.stop - keys.start
                        product(out[:, 0:n], [(qT[part, h, tile(t)], kT[part, h, keys])], True)
                    for u in turned:
                        n = 1 if units[u][1] == 0 else 3
                        out = opened(("pT", l, u))
                        is_read(pe, ("S", l, u))
                        turn(out, [pbuf[:, u % 4, tile(j)] for j in range(n)])
                    for u in outs:
                        h, t, m = units[u]
                        tiles = [0] if t == 0 else [1, 2, 3]
                        out = opened(("o", l, u))
                        is_read(pe, ("pT", l, u))
                        v = v_e if l == 0 else v_o
                        w = NOPE if l == 0 else DV
                        product(out[:, 0:w], [(pTbuf[:, u % 4, j, :], v[:, s, w * h:w * h + w]) for j, s in enumerate(tiles)], True)
                    if sums:
                        ada_sums(*sums)
                    if columns:
                        ada_columns(*columns)

            def mixer_out(l):
                order = [4, 5, 6, 7, 0, 1, 2, 3] if l == 0 else list(range(KD))

                def mixed(k):
                    c = order[k]
                    if l == 0 and c < NCH:
                        pe.wait_ge(sem("conv_out"), 2 * c + 2)
                    else:
                        is_read(pe, ("oT", l, c - NCH if l == 0 else c))

                if l == 0:
                    is_read(pe, ("o", l, NT * HEADS - 1))
                    for j in range(NCH):
                        turn(opened(("oT", l, j)), [o_e[:, t, P * j:P * j + P] for t in range(NT)])
                    out = opened("conv_mean")
                    pe.wait_ge(sem("conv_ready"), 1)
                    product(out[:, 0:CONVO], [(ones[:, :], conv_acc[:, j, :]) for j in range(NCH)], True)
                    out = opened("conv_var")
                    pe.wait_ge(sem("conv_squares"), NCH)
                    product(out[:, 0:CONVO], [(ones[:, :], conv_sq[:, j, :]) for j in range(NCH)], True)
                else:
                    pe.wait_ge(sem("o_normed"), 1)
                    for j in range(KD):
                        turn(opened(("oT", l, j)), [o_o[:, t, P * j:P * j + P] for t in range(NT)])
                for b in range(4):
                    w = arrived("w_o", l, b).rearrange("p (k n) -> p k n", k=KD)
                    for c in range(2):
                        product(opened(("out", l, 2 * b + c))[:, 0:TOK],
                                [(w[:, k, P * c:P * c + P], hT[:, k, :]) for k in order], True,
                                mixed if b == 0 and c == 0 else None)

            def routing(l):
                out = opened(("router", l))
                pe.wait_ge(sem("router_loaded"), 64)
                for t in range(NT):
                    product(out[:, (NG + NE) * t:(NG + NE) * (t + 1)],
                            [(hT[:, k, tile(t)], wr[:, l, k, :]) for k in range(KD)], t == NT - 1,
                            chunk_of_h(2 * l + 1) if t == 0 else None)
                for t in range(NT):
                    for b in range(2):
                        turn(opened(("htok", l, t, b)), [hT[:, 4 * b + j, tile(t)] for j in range(4)])
                out = opened(("rank", l))
                pe.wait_ge(sem("chosen"), l + 1)
                m = rt[:, M_BOTH, :].rearrange("p (t e) -> p t e", t=NT)
                for t in range(NT):
                    product(out[:, NE * t:NE * t + NE], [(ones[:, :], m[:, s, :]) for s in range(t)] + [(below[:, :], m[:, t, :])])
                product(out[:, NE * NT:NE * NT + NE], [(ones[:, :], m[:, s, :]) for s in range(NT)], True)
                pe.wait_ge(sem("diagonals_ready"), l + 1)
                for i in range(NT):
                    product(opened(("codes", l, i)), [(ones[:, :], diagonals[:, 4 * i:4 * i + 4, :])], True)

            def experts(l):
                base = NE * l

                def await_rows(n, t=0):
                    b = n % BUFFERS
                    pe.wait_ge(sem(f"rows{b}_loaded"), 16 * ((base + n) // BUFFERS + 1) + 16 * (UNROLL // BUFFERS) * t)
                    if base + n:
                        pe.wait_ge(sem("rowsT_ready"), UNROLL * t + (base + n))

                def rows_turn(n):
                    b = n % BUFFERS
                    for c in range(KD):
                        mm = pe.transpose(bank[0][:, ROWS * c:ROWS * c + ROWS], te[b][:, c:D:KD], ident[0:ROWS, 0:ROWS])
                    mm.then_inc(sem("rows_turned"), 1)

                def gate_up(n, t=0):
                    w = []
                    for k in range(2):
                        i = expert_piece(l, n, k)
                        pe.wait_ge(slot_sem(i), landed(i) + 16 * (UNROLL // BUFFERS) * t)
                        w.append(slot(i).rearrange("p (k n) -> p k n", k=KD))
                    pe.wait_ge(sem("rowsT_ready"), UNROLL * t + (base + n + 1))
                    if base + n:
                        pe.wait_ge(sem("hid_ready"), UNROLL * t + (base + n))
                    for c in range(KD):
                        for k in range(2):
                            mm = pe.matmul(bank[1][ROWS * k:ROWS * k + ROWS, 0:FF], teT[n % BUFFERS][:, c, :], w[k][:, c, :],
                                           start=(c == 0), stop=(c == KD - 1), tile_position=(0, ROWS * k))
                    mm.then_inc(sem("gate_up_filled"), 1)

                def await_hid(n, t=0):
                    pe.wait_ge(sem("hid_ready"), UNROLL * t + (base + n + 1))
                    if base + n:
                        pe.wait_ge(sem("hidT_ready"), UNROLL * t + (base + n))

                def hid_turn(n):
                    for j in range(2):
                        mm = pe.transpose(bank[2][:, ROWS * j:ROWS * j + ROWS], hid[:, n % BUFFERS, j:FF:2], ident[0:ROWS, 0:ROWS])
                    mm.then_inc(sem("hid_turned"), 1)

                def down(n, t=0):
                    i = expert_piece(l, n, 2)
                    pe.wait_ge(slot_sem(i), landed(i) + 16 * (UNROLL // BUFFERS) * t)
                    pe.wait_ge(sem("hidT_ready"), UNROLL * t + (base + n + 1))
                    if base + n:
                        pe.wait_ge(sem("y_copied"), UNROLL * t + (base + n))
                    for j in range(2):
                        for b in range(2):
                            mm = pe.matmul(bank[3][ROWS * b:ROWS * b + ROWS, :], hidT[:, n % BUFFERS, j, :],
                                           slot(i)[:, D * j + 512 * b:D * j + 512 * b + 512], start=(j == 0), stop=(j == 1),
                                           tile_position=(0, ROWS * b))
                    mm.then_inc(sem("down_filled"), 1)

                def spread_out(q, rounds, t=0):
                    q_all, bodies = NE // 2 * l + q, UNROLL // 2 * t
                    if rounds[0] == 0:
                        pe.wait_ge(sem("y_copied"), UNROLL * t + (2 * q_all + 2))
                        pe.wait_ge(sem("weights_placed"), bodies + (q_all + 1))
                    for r in rounds:
                        if PAIR_ROUNDS * q_all + r > 1:
                            pe.wait_ge(sem("spread_added"), PAIR_ROUNDS * bodies + (PAIR_ROUNDS * q_all + r - 1))
                        for i in range(2):
                            mm = pe.matmul(bank[4 + 2 * (r % 2) + i][:, 0:TOK], y_pair[q % BUFFERS][:, P * (2 * r + i):P * (2 * r + i + 1)],
                                           weights_at[q % BUFFERS], start=True, stop=True)
                        mm.then_inc(sem("spread_filled"), 1)

                def step(n, t=0):
                    await_hid(n - 1, t)
                    if n < NE - 1:
                        await_rows(n + 1, t)
                    gate_up(n, t)
                    hid_turn(n - 1)
                    if n < NE - 1:
                        rows_turn(n + 1)
                    if n >= 3:
                        spread_out((n - 3) // 2, ((0, 1), (2, 3))[(n - 3) % 2], t)
                    down(n - 1, t)

                for name in groups.names[at[0] - 8:at[0]]:
                    is_read(pe, name)
                await_rows(0)
                rows_turn(0)
                gate_up(0)
                await_rows(1)
                rows_turn(1)
                for n in range(1, STEPS_AHEAD + 1):
                    step(n)
                with pe.Fori(0, BODIES) as t:
                    for n in range(STEPS_AHEAD + 1, STEPS_AHEAD + 1 + UNROLL):
                        step(n, t)
                for n in range(STEPS_AHEAD + 1 + UNROLL * BODIES, NE):
                    step(n)
                await_hid(NE - 1)
                hid_turn(NE - 1)
                spread_out(NE // 2 - 2, (2, 3))
                down(NE - 1)
                spread_out(NE // 2 - 1, (0, 1, 2, 3))
                pe.wait_ge(sem("spread_added"), PAIR_ROUNDS * NE // 2 * (l + 1))

                def further_turn(i):
                    pe.wait_ge(sem(f"further{l}_loaded"), 64 * i + 64)
                    for c in range(KD):
                        mm = pe.matmul(bank[0][:, ROWS * c:ROWS * c + ROWS], te[0][:, c:D:KD], ident[0:ROWS, 0:ROWS], start=True, stop=True)
                    mm.then_inc(sem(f"further{l}_rows_turned"), 1)
                    pe.wait_ge(sem(f"further{l}_rowsT"), i + 1)
                    for k in range(2):
                        w = ring[:, k, :].rearrange("p (k n) -> p k n", k=KD)
                        for c in range(KD):
                            mm = pe.matmul(bank[1 + k][0:ROWS, 0:FF], teT[0][:, c, :], w[:, c, :], start=(c == 0), stop=(c == KD - 1))
                    mm.then_inc(sem(f"further{l}_up"), 1)
                    pe.wait_ge(sem(f"further{l}_hid"), i + 1)
                    for j in range(2):
                        mm = pe.matmul(bank[3][:, ROWS * j:ROWS * j + ROWS], hid[:, 0, j:FF:2], ident[0:ROWS, 0:ROWS], start=True, stop=True)
                    mm.then_inc(sem(f"further{l}_hid_turned"), 1)
                    pe.wait_ge(sem(f"further{l}_hidT"), i + 1)
                    for b in range(2):
                        for j in range(2):
                            mm = pe.matmul(bank[4 + b][0:ROWS, :], hidT[:, 0, j, :], ring[:, 2, D * j + 512 * b:D * j + 512 * b + 512],
                                           start=(j == 0), stop=(j == 1))
                    mm.then_inc(sem(f"further{l}_down"), 1)
                    pe.wait_ge(sem(f"further{l}_y"), i + 1)
                    for r in range(PAIR_ROUNDS):
                        if r:
                            pe.wait_ge(sem(f"further{l}_added"), PAIR_ROUNDS * i + r)
                        for k in range(2):
                            mm = pe.matmul(bank[6 + k][:, 0:TOK], y_further[:, P * (2 * r + k):P * (2 * r + k + 1)],
                                           weights_at[0][0:ROWS, :], start=True, stop=True)
                        mm.then_inc(sem(f"further{l}_spread"), 1)

                further_turns(pe, l, further_turn, (f"further{l}_added", PAIR_ROUNDS * (ROUNDS - 1) * NE))

            def final(t):
                pe.wait_ge(sem("experts_added"), 2 * KD + KD * min(t + 1, 2))
                for b in range(2):
                    out = opened(("final", t, b))
                    turn(out, [xT[:, 4 * b + j, tile(t)] for j in range(4)])

            pe.wait_ge(sem("constants_ready"), 1)
            pe.wait_ge(sem("vectors_loaded"), 16 * 10)
            turn(opened("vectors"), [packs[:, i, :] if i < 2 else packs[0:NCOL - 2 * P, 2, :] for i in range(3)])
            pe.wait_ge(sem("x_loaded"), 48)
            for c in range(KD):
                turn(opened(("xT", c)), [xtok[:, t, P * c:P * c + P] for t in range(NT)])
            sum_of_squares(0, 0)
            pe.wait_ge(sem("cond_ready"), 1)
            for s in range(2):
                ada_sums(0, s)
                ada_columns(0, s)
            for l in range(DEPTH):
                if l == 0:
                    even_projections()
                else:
                    sum_of_squares(l, 0)
                    odd_projections()
                turned_heads(l)
                attention(l)
                mixer_out(l)
                sum_of_squares(l, 1)
                routing(l)
                experts(l)
            for t in range(NT):
                final(t)

        @block.scalar
        def _(act):
            step = [0]

            def link(ins):
                step[0] += 1
                ins.then_inc(sem("scalar_step"), 1)
                act.wait_ge(sem("scalar_step"), step[0])

            def done(ins):
                ins.then_inc(sem("read_by_scalar"), 1)

            def squares(l, w):
                for c in range(KD):
                    if l or w:
                        if w == 0:
                            act.wait_ge(sem("experts_added"), 2 * KD * (l - 1) + 2 * c + 2)
                        else:
                            is_read(act, ("out", l, c))
                    act.activation(scratch[:, c * TOK:c * TOK + TOK], xT[:, c, :], ACT.Square).then_inc(sem("squares_ready"), 1)

            def modulated(l, w):
                is_filled(act, ("sumsq", l, w))
                done(act.activation(std[:, 0:TOK], psum(("sumsq", l, w))[:, 0:TOK], ACT.Sqrt, scale=1.0 / D, bias=eps[:, 0:1]))
                if l == 0 and w == 0:
                    for s in range(2):
                        ada_copy(0, s)
                is_read(act, ("adaT", l, 3 * w + 1))
                act.wait_ge(sem("scales_ready"), 2 * l + w + 1)
                for c in range(KD):
                    act.wait_ge(sem("hn_ready"), KD * (2 * l + w) + c + 1)
                    act.activation(hT[:, c, CTX:], hn[:, c, CTX:], ACT.Identity, scale=mcol(l, 3 * w + 1, c, 1),
                                   bias=mcol(l, 3 * w, c, 1)).then_inc(sem("h_lat_ready"), 1)

            def ada_copy(l, s):
                is_filled(act, ("ada", l, s))
                if (l, s) != (0, 0):
                    is_filled(act, ("adaT", l, s - 1) if s else ("adaT", 0, 5))
                done(act.activation(ada_rows[:, :], psum(("ada", l, s)), ACT.Copy))

            def head_std(l, i, buf, rows, width, view=None):
                act.activation(scratch[:, 0:rows * width], buf, ACT.Square).then_inc(sem("head_squares"), 1)
                act.wait_ge(sem("head_sums"), i + 1)
                act.activation(small[:, 2 * (i % 4) + 1, 0:rows], small[:, 2 * (i % 4), 0:rows], ACT.Sqrt,
                               scale=1.0 / width, bias=eps[:, 0:1]).then_inc(sem("head_stds"), 1)

            def experts(l):
                base = NE * l

                def silu(n, t=0):
                    act.wait_ge(sem("gate_up_filled"), UNROLL * t + (base + n + 1))
                    if base + n >= BUFFERS:
                        act.wait_ge(sem("hid_ready"), UNROLL * t + (base + n - 1))
                    act.activation(sgate[:, n % BUFFERS, :], bank[1][0:ROWS, 0:FF], ACT.Silu).then_inc(sem("silu_done"), 1)

                def hid_copy(n, t=0):
                    act.wait_ge(sem("hid_turned"), UNROLL * t + (base + n + 1))
                    act.activation(hidT[:, n % BUFFERS, :, :].rearrange("p j r -> p (j r)"), bank[2][:, 0:2 * ROWS],
                                   ACT.Copy).then_inc(sem("hidT_ready"), 1)

                def y_copy(n, t=0):
                    act.wait_ge(sem("down_filled"), UNROLL * t + (base + n + 1))
                    before = NE // 2 * l + n // 2 - 1
                    if before > 0:
                        act.wait_ge(sem("spread_filled"), PAIR_ROUNDS * (UNROLL // 2) * t + PAIR_ROUNDS * before)
                    rows = slice(ROWS * (n % 2), ROWS * (n % 2) + ROWS)
                    act.activation(y_pair[n // 2 % BUFFERS][rows, 0:512], bank[3][0:ROWS, :], ACT.Copy)
                    act.activation(y_pair[n // 2 % BUFFERS][rows, 512:D], bank[3][ROWS:2 * ROWS, :], ACT.Copy).then_inc(sem("y_copied"), 1)

                def step(n, t=0):
                    silu(n, t)
                    hid_copy(n - 1, t)
                    y_copy(n - 1, t)

                silu(0)
                for n in range(1, STEPS_AHEAD + 1):
                    step(n)
                with act.Fori(0, BODIES) as t:
                    for n in range(STEPS_AHEAD + 1, STEPS_AHEAD + 1 + UNROLL):
                        step(n, t)
                for n in range(STEPS_AHEAD + 1 + UNROLL * BODIES, NE):
                    step(n)
                hid_copy(NE - 1)
                y_copy(NE - 1)

                def further_turn(i):
                    act.wait_ge(sem(f"further{l}_up"), i + 1)
                    act.activation(sgate[:, 0, :], bank[1][0:ROWS, 0:FF], ACT.Silu).then_inc(sem(f"further{l}_silu"), 1)
                    act.wait_ge(sem(f"further{l}_hid_turned"), i + 1)
                    act.activation(hidT[:, 0, :, :].rearrange("p j r -> p (j r)"), bank[3][:, 0:2 * ROWS],
                                   ACT.Copy).then_inc(sem(f"further{l}_hidT"), 1)

                further_turns(act, l, further_turn)

            act.dma_start(xtok[:, 0, :], x_prompt[0]).then_inc(sem("x_loaded"), 16)
            for t in range(2):
                act.dma_start(xtok[:, 1 + t, :], x_sample[0, P * t:P * t + P, :]).then_inc(sem("x_loaded"), 16)
            is_read(act, "vectors")
            act.wait_ge(sem("constants_ready_v"), 1)
            for j, at in ((0, C_CCTX), (1, C_COND)):
                ins = act.activation(condS[:, :, j], cols[:, at:at + KD], ACT.Silu)
            ins.then_inc(sem("cond_ready"), 1)
            for c in range(KD):
                is_filled(act, ("xT", c))
                done(act.activation(xT[:, c, :], psum(("xT", c))[:, 0:TOK], ACT.Copy))
            act.wait_ge(sem("read_by_scalar"), groups.count[groups.at[("xT", KD - 1)]])
            for l in range(DEPTH):
                squares(l, 0)
                modulated(l, 0)
                if l == 0:
                    act.wait_ge(sem("lambda_sums"), 1)
                    act.activation(lam[:, 2:4], lam[:, 0:2], ACT.Exp).then_inc(sem("lambda_exps"), 1)
                    for i, (kind, js) in enumerate(IN_BLOCKS):
                        if kind == "rest":
                            width = min(256, REST - 256 * js)
                            for t in range(NT):
                                is_filled(act, ("rest", js, t))
                                done(act.activation(proj[:, t, 256 * js:256 * js + width], psum(("rest", js, t))[:, 0:width], ACT.Copy))
                        else:
                            for j in js:
                                is_filled(act, (kind, j))
                                dst, f = (glu_a, ACT.Copy) if kind == "glu_a" else (glu_g, ACT.Sigmoid)
                                done(act.activation(dst[:, j, :], psum((kind, j))[:, 0:TOK], f))
                        if i in ADA_AFTER_BLOCK:
                            ada_copy(*ADA_AFTER_BLOCK[i])
                    act.wait_ge(sem("read_by_scalar"), groups.count[groups.at[("rest", 2, 2)]])
                    act.wait_ge(sem("u_ready"), 2 * NCH)
                    for t in range(NT):
                        for i, (a, n) in enumerate(((0, QR), (QR, KVR))):
                            link(act.activation(scratch[:, 0:n], proj[:, t, a:a + n], ACT.Square, scale=float(n) ** -0.5,
                                                accum_out=small[:, 6, 2 * t + i:2 * t + i + 1]))
                    act.activation(small[:, 7, 0:2 * NT], small[:, 6, 0:2 * NT], ACT.Sqrt, bias=eps[:, 0:1]).then_inc(sem("latent_std"), 1)
                    for j in range(3):
                        is_filled(act, ("qanT", j))
                        done(act.activation(qanT[:, j, :], psum(("qanT", j))[:, 0:TOK], ACT.Identity, scale=col(C_QRG + j)))
                    is_read(act, ("q", 1, 2))
                    head_std(l, 0, q_e.rearrange("p t n -> p (t n)"), NT * HEADS, QK)
                    act.wait_ge(sem("pad_stored"), 16)
                    for t in range(NT + 1):
                        for b in range(2):
                            is_filled(act, ("kv", t, b))
                            src = psum(("kv", t, b)).rearrange("p (h e) -> p h e", h=4)
                            act.activation(k_e[:, t, 4 * b:4 * b + 4, 0:NOPE], src[:, :, 0:NOPE], ACT.Copy)
                            done(act.activation(v_e[:, t, 256 * b:256 * b + 256].rearrange("p (h e) -> p h e", h=4),
                                                src[:, :, NOPE:], ACT.Copy))
                    act.wait_ge(sem("k_rope_placed"), 4)
                    act.wait_ge(sem("read_by_scalar"), groups.count[groups.at[("kv", 3, 1)]])
                    head_std(l, 1, k_e.rearrange("p t h e -> p (t h e)"), 4 * HEADS, QK)
                else:
                    for b in range(12):
                        for t in range(NT):
                            if (b * NT + t) % 2 == 0:
                                is_filled(act, ("qkv", b, t))
                                dst = (q_o, k_o, v_o)[b // 4]
                                done(act.activation(dst[:, t, 256 * (b % 4):256 * (b % 4) + 256], psum(("qkv", b, t))[:, 0:256], ACT.Copy))
                        if b in (4, 8):
                            is_read(act, ("qkv", b - 1, 2))
                            is_read(act, ("qkv", b - 1, 1))
                            buf = (q_o if b == 4 else k_o[:, 0:NT, :]).rearrange("p t n -> p (t n)")
                            head_std(l, 1 + b // 4, buf, NT * 2 * HEADS, DK)
                for h in range(HEADS):
                    is_filled(act, ("qT", l, h))
                    n = QK if l == 0 else P
                    done(act.activation(qT[0:n, h, :], psum(("qT", l, h))[0:n, 0:TOK], ACT.Copy))
                units = attention_units(l)
                first = (0, len(attention_units(0)))[l]
                for scores, turned, outs, sums, columns in attention_steps(l):
                    for u in scores:
                        n = P if units[u][1] == 0 else 3 * P
                        act.wait_ge(sem("negmax_ready"), first + u + 1)
                        if u >= 4:
                            is_filled(act, ("pT", l, u - 4))
                        done(act.activation(pbuf[:, u % 4, 0:n], psum(("S", l, u))[:, 0:n], ACT.Exp, bias=negmax[:, u:u + 1],
                                            accum_out=rowsum[:, u:u + 1]))
                    for u in turned:
                        n = 1 if units[u][1] == 0 else 3
                        is_filled(act, ("pT", l, u))
                        if u >= 4:
                            is_filled(act, ("o", l, u - 4))
                        done(act.activation(pTbuf[:, u % 4, 0:n, :].rearrange("p a b -> p (a b)"), psum(("pT", l, u))[:, 0:n * P], ACT.Copy))
                    if sums:
                        ada_copy(*sums)
                if l == 1:
                    is_read(act, ("o", l, len(units) - 1))
                    head_std(l, 4, o_o.rearrange("p t n -> p (t n)"), NT * HEADS, DV)
                for j in range((NCH, KD)[l]):
                    is_filled(act, ("oT", l, j))
                    done(act.activation(hT[:, (NCH, 0)[l] + j, :], psum(("oT", l, j))[:, 0:TOK], ACT.Copy))
                if l == 0:
                    is_read(act, "conv_mean")
                    for j in range(NCH):
                        act.activation(conv_sq[:, j, :], conv_acc[:, j, :], ACT.Square).then_inc(sem("conv_squares"), 1)
                    is_filled(act, "conv_var")
                    done(act.activation(std[:, :], psum("conv_var")[:, 0:CONVO], ACT.Sqrt, scale=1.0 / CH, bias=eps[:, 0:1]))
                    for j in range(NCH):
                        act.wait_ge(sem("conv_normed"), j + 1)
                        for a, b, src in ((0, CTX, 0), (CTX, TOK, CTX + PADC)):
                            act.activation(hT[:, j, a:b], conv_acc[:, j, src:src + b - a], ACT.Silu, scale=col(C_LNG + j),
                                           bias=col(C_LNB + j)).then_inc(sem("conv_out"), 1)
                squares(l, 1)
                modulated(l, 1)
                for t in range(NT):
                    for b in range(2):
                        is_filled(act, ("htok", l, t, b))
                        done(act.activation(htok[:, t, 512 * b:512 * b + 512], psum(("htok", l, t, b)), ACT.Copy))
                for i, (src, dst, n) in enumerate(((gsub, gexp, NT * NG), (rs[:, R_D, :], rs[:, R_ED, :], NT))):
                    act.wait_ge(sem("exp_asked"), 2 * l + i + 1)
                    act.activation(dst, src, ACT.Exp).then_inc(sem("exp_given"), 1)
                for i in range(NT):
                    is_filled(act, ("codes", l, i))
                    done(act.activation(pair_rows[:, 512 * i:512 * i + 512], psum(("codes", l, i)), ACT.Copy))
                experts(l)
            act.wait_ge(sem("cache_stored"), 64)
            for t in range(NT):
                is_filled(act, ("final", t, 0))
                done(act.activation(xout[:, t, 0:512], psum(("final", t, 0)), ACT.Copy))

        @block.vector
        def _(ve):
            step = [0]

            def mark(ins):
                step[0] += 1
                ins.then_inc(sem("vector_step"), 1)
                return step[0]

            def link(ins):
                ve.wait_ge(sem("vector_step"), mark(ins))

            def done(ins):
                ins.then_inc(sem("read_by_vector"), 1)

            def over(ap, n):
                return ap.unsqueeze(len(ap.shape)).to_broadcast(tuple(ap.shape) + (n,))

            def scaled(out, a, b, op=ALU.mult):
                return ve.tensor_tensor(out=out, in0=a, in1=b, op=op)

            def ada_columns(l, s):
                is_filled(ve, ("adaT", l, s))
                b = cols[:, C_ADA + 48 * l + KD * s:C_ADA + 48 * l + KD * s + KD]
                done(scaled(mod[:, l, s, :, :], psum(("adaT", l, s))[:, 0:2 * KD].rearrange("p (n j) -> p n j", j=2),
                            over(b, 2), ALU.add))
                if s % 3 == 1:
                    is_read(ve, ("adaT", l, s))
                    a = (C_N1 if s == 1 else C_N2) + KD * l
                    ve.scalar_tensor_tensor(out=mod[:, l, s, :, :], in0=mod[:, l, s, :, :], scalar=1.0,
                                            in1=over(cols[:, a:a + KD], 2), op0=ALU.add, op1=ALU.mult).then_inc(sem("scales_ready"), 1)

            def normed(l, w):
                is_read(ve, ("sumsq", l, w))
                link(ve.reciprocal(rstd[:, 0:TOK], std[:, 0:TOK]))
                for c in range(KD):
                    scaled(hn[:, c, :], xT[:, c, :], rstd[:, 0:TOK]).then_inc(sem("hn_ready"), 1)

            def conv_taps():
                for pair in ((0, 1), (2, 3)):
                    before = [0, 0]
                    for k in range(TAPS):
                        for i, j in enumerate(pair):
                            src = uT[:, j, k:k + CONVO]
                            w = col(C_CW + NCH * k + j)
                            if k == 0:
                                ins = ve.tensor_scalar(conv_acc[:, j, :], src, w, col(C_CB + j), ALU.mult, ALU.add)
                            else:
                                ve.wait_ge(sem("vector_step"), before[i])
                                ins = ve.scalar_tensor_tensor(out=conv_acc[:, j, :], in0=src, scalar=w, in1=conv_acc[:, j, :],
                                                              op0=ALU.mult, op1=ALU.add)
                            before[i] = mark(ins)
                        yield k

            def head_norm(i, buf, rows, width, gain, ready):
                k = 2 * (i % 4)
                ve.wait_ge(sem("head_squares"), i + 1)
                ve.tensor_reduce(out=small[:, k, 0:rows], in_=scratch[:, 0:rows * width].rearrange("p (r e) -> p r e", e=width),
                                 axis=AX.X, op=ALU.add).then_inc(sem("head_sums"), 1)
                ve.wait_ge(sem("head_stds"), i + 1)
                link(ve.reciprocal(small[:, k + 1, 0:rows], small[:, k + 1, 0:rows]))
                link(scaled(buf, buf, over(small[:, k + 1, 0:rows], width)))
                scaled(buf, buf, gain.unsqueeze(1).to_broadcast((P, rows, width))).then_inc(sem(ready), 1)

            def mixer_residual(l):
                for c in range(KD):
                    is_filled(ve, ("out", l, c))
                    for a, b, j in SEG:
                        ins = ve.scalar_tensor_tensor(out=xT[:, c, a:b], in0=psum(("out", l, c))[:, a:b], scalar=mcol(l, 2, c, j),
                                                      in1=xT[:, c, a:b], op0=ALU.mult, op1=ALU.add)
                    done(ins)

            def expert_residual(l):
                parts = [(c, seg) for c in range(KD) for seg in SEG]
                if l == DEPTH - 1:
                    parts.sort(key=lambda part: part[1][0])
                for c, (a, b, j) in parts:
                    ve.scalar_tensor_tensor(out=xT[:, c, a:b], in0=moe_sum[:, c, a:b], scalar=mcol(l, 5, c, j),
                                            in1=xT[:, c, a:b], op0=ALU.mult, op1=ALU.add).then_inc(sem("experts_added"), 1)

            def attention(l, taps):
                units = attention_units(l)
                for scores, turned, outs, sums, columns in attention_steps(l):
                    for u in scores:
                        n = P if units[u][1] == 0 else 3 * P
                        is_filled(ve, ("S", l, u))
                        ve.tensor_reduce(out=negmax[:, u:u + 1], in_=psum(("S", l, u))[:, 0:n], axis=AX.X, op=ALU.max,
                                         negate=True).then_inc(sem("negmax_ready"), 1)
                    next(taps, None)
                    for u in outs:
                        h, t, m = units[u]
                        is_read(ve, ("S", l, u))
                        link(ve.reciprocal(rinv[:, u:u + 1], rowsum[:, u:u + 1]))
                        if m == 0:
                            w = NOPE if l == 0 else DV
                            dst = (o_e if l == 0 else o_o)[:, t, w * h:w * h + w]
                            is_filled(ve, ("o", l, u))
                            done(ve.tensor_scalar(dst, psum(("o", l, u))[:, 0:w], rinv[:, u:u + 1], None, ALU.mult))
                        else:
                            link(scaled(rinv[:, u:u + 1], rinv[:, u:u + 1], lam[:, 5:6]))
                            dst = o_o[:, t, DV * h:DV * h + DV]
                            is_filled(ve, ("o", l, u))
                            is_read(ve, ("o", l, u - 1))
                            done(ve.scalar_tensor_tensor(out=dst, in0=psum(("o", l, u))[:, 0:DV], scalar=rinv[:, u:u + 1],
                                                         in1=dst, op0=ALU.mult, op1=ALU.add))
                    if columns:
                        ada_columns(*columns)
                for _ in taps:
                    pass

            def routing(l):
                k = B_MOE + (NG + NE) * l
                is_filled(ve, ("router", l))
                done(scaled(logits[:, :, :], psum(("router", l))[:, 0:NT * (NG + NE)].rearrange("p (t e) -> p t e", t=NT),
                            bc[:, k:k + NG + NE].unsqueeze(1).to_broadcast((P, NT, NG + NE)), ALU.add))
                is_read(ve, ("router", l))

                def m(i):
                    return rt[:, i, :].rearrange("p (t e) -> p t e", t=NT)

                def g(ap):
                    return ap.rearrange("p (t e) -> p t e", t=NT)

                def r(i):
                    return rs[:, i, :]

                def top(out, src, op=ALU.max):
                    link(ve.tensor_reduce(out=out, in_=src, axis=AX.X, op=op))

                def first_of_equals(one, src, value, eq, rank, best, n):
                    link(scaled(eq, src, over(r(value), n), ALU.is_equal))
                    link(scaled(rank, eq, ramp[:, NE - n:NE].unsqueeze(1).to_broadcast((P, NT, n))))
                    top(r(best), rank)
                    link(scaled(one, rank, over(r(best), n), ALU.is_equal))

                gl, el = logits[:, :, 0:NG], logits[:, :, NG:]
                top(r(R_GMAX), gl)
                scaled(g(gsub), gl, over(r(R_GMAX), NG), ALU.subtract).then_inc(sem("exp_asked"), 1)
                first_of_equals(g(gone), gl, R_GMAX, g(geq), g(grank), R_GTOP, NG)
                link(ve.tensor_scalar(g(gpen), g(gone), BIG, -BIG, ALU.mult, ALU.add))
                link(scaled(rt[:, M_SEL, :].rearrange("p (t g e) -> p t g e", t=NT, g=NG),
                            el.rearrange("p t (g e) -> p t g e", g=NG), over(g(gpen), EPG), ALU.add))
                top(r(R_M1), m(M_SEL))
                first_of_equals(m(M_ONE1), m(M_SEL), R_M1, m(M_EQ), m(M_WORK), R_TOP1, NE)
                link(ve.scalar_tensor_tensor(out=m(M_SEL2), in0=m(M_ONE1), scalar=-BIG, in1=m(M_SEL), op0=ALU.mult, op1=ALU.add))
                top(r(R_M2), m(M_SEL2))
                scaled(r(R_D), r(R_M2), r(R_M1), ALU.subtract).then_inc(sem("exp_asked"), 1)
                first_of_equals(m(M_ONE2), m(M_SEL2), R_M2, m(M_EQ), m(M_WORK), R_TOP2, NE)
                scaled(m(M_BOTH), m(M_ONE1), m(M_ONE2), ALU.add).then_inc(sem("chosen"), 1)
                ve.wait_ge(sem("exp_given"), 2 * l + 2)
                top(r(R_GSUM), g(gexp), ALU.add)
                link(ve.tensor_scalar(r(R_D), r(R_ED), 1.0, None, ALU.add))
                link(scaled(r(R_GATE), r(R_GSUM), r(R_D)))
                link(ve.reciprocal(r(R_W1), r(R_GATE)))
                link(scaled(r(R_W2), r(R_W1), r(R_ED)))
                is_filled(ve, ("rank", l))
                pr = psum(("rank", l))
                count = pr[:, NE * NT:NE * NT + NE]
                link(ve.tensor_copy(prefix[:, 0, 16:], count))
                a = 0
                for d in (1, 2, 4, 8, 16):
                    link(scaled(prefix[:, 1 - a, 16:], prefix[:, a, 16:], prefix[:, a, 16 - d:16 - d + NE], ALU.add))
                    a = 1 - a
                link(scaled(prefix[:, a, 16:], prefix[:, a, 16:], pr[:, NE * NT:NE * NT + NE], ALU.subtract))
                if l:
                    ve.wait_ge(sem("rows_turned"), NE)
                first = rt[:, M_RANK - 1:M_RANK + 1, :].rearrange("p a (j e) -> p (a j) e", e=NE)
                link(scaled(first, prefix[:, a, 16:].unsqueeze(1).to_broadcast((P, ROUNDS, NE)), over(turn_row[:, 0:ROUNDS], NE), ALU.add))
                link(ve.tensor_scalar(starts[:, :].rearrange("p (j e) -> p j e", e=NE), first, float(PAIRS), None, ALU.min))
                top(rs[:, R_TURN, 0:1], count)
                ve.tensor_scalar(overflow[:, l:l + 1], rs[:, R_TURN, 0:1], float(ROWS), None, ALU.is_gt).then_inc(sem("starts_ready"), 1)
                link(ve.tensor_copy(rt[:, M_RANK, :], pr[:, 0:NE * NT]))
                done(scaled(m(M_PLACE), pr[:, 0:NE * NT].rearrange("p (t e) -> p t e", t=NT),
                            prefix[:, a, 16:].unsqueeze(1).to_broadcast((P, NT, NE)), ALU.add))
                is_read(ve, ("rank", l))
                def both(i):
                    return rt[:, i:i + 2, :].rearrange("p k (t e) -> p k t e", t=NT)

                for what, into in ((M_PLACE, R_P1), (M_RANK, R_RANK1), (None, R_ID1)):
                    w = m(what) if what is not None else turn_row[:, :].unsqueeze(1).to_broadcast((P, NT, NE))
                    link(scaled(both(M_WORK), both(M_ONE1), w.unsqueeze(1).to_broadcast((P, 2, NT, NE))))
                    top(rs[:, into:into + 2, :], both(M_WORK), ALU.add)
                ins = ve.tensor_copy(idx_sorted[:, :], rs[:, R_P1:R_P2 + 1, :].rearrange("p k t -> p (k t)"))
                ins.then_inc(sem("places_ready"), 1)
                ve.wait_ge(sem("places_ready"), l + 1)
                ids = rs[:, R_ID1:R_ID2 + 1, :].rearrange("p k t -> p (k t)")
                ranks = rs[:, R_RANK1:R_RANK2 + 1, :].rearrange("p k t -> p (k t)")
                late = rt[:, M_WORK, 0:2 * NT * (ROUNDS - 1)].rearrange("p (i j) -> p i j", j=ROUNDS - 1)
                link(scaled(late, over(ranks, ROUNDS - 1), turn_row[:, 1:ROUNDS].unsqueeze(1).to_broadcast((P, 2 * NT, ROUNDS - 1)), ALU.is_ge))
                places = rs[:, R_P1:R_P2 + 1, :].rearrange("p k t -> p (k t)")
                top(places, late, ALU.add)
                link(scaled(ids, ids, ranks, ALU.add))
                link(ve.scalar_tensor_tensor(out=ids, in0=places, scalar=float(NE * ROWS - ROWS), in1=ids, op0=ALU.mult, op1=ALU.add))
                scaled(diagonals, ident[:, :].unsqueeze(1).to_broadcast((P, 4 * NT, P)),
                       over(rs[:, R_ID1:R_ID1 + 4, :].rearrange("p k t -> p (k t)"), P)).then_inc(sem("diagonals_ready"), 1)
                ve.tensor_scalar(pair_codes, turn_row[:, 0:NE:2], row_of[:, 0:1], None, ALU.add).then_inc(sem("pair_codes_ready"), 1)

            def experts(l):
                base = NE * l

                def rows_copy(n, t=0):
                    ve.wait_ge(sem("rows_turned"), UNROLL * t + (base + n + 1))
                    ve.tensor_copy(teT[n % BUFFERS].rearrange("p c r -> p (c r)"), bank[0][:, :]).then_inc(sem("rowsT_ready"), 1)

                def hidden(n, t=0):
                    ve.wait_ge(sem("silu_done"), UNROLL * t + (base + n + 1))
                    scaled(hid[:, n % BUFFERS, :], sgate[:, n % BUFFERS, :], bank[1][ROWS:2 * ROWS, 0:FF]).then_inc(sem("hid_ready"), 1)

                def place_weights(q, t=0):
                    count = UNROLL // 2 * t + (NE // 2 * l + q)
                    if NE // 2 * l + q:
                        ve.wait_ge(sem("weights_placed"), count)
                    place(weights_at[q % BUFFERS], pair_codes[:, bass.ds(UNROLL // 2 * t + q, 1)],
                          sem("choices_placed"), count + 1, sem("weights_placed"))

                def place(out, code, half_way, count, ready):
                    ve.scalar_tensor_tensor(out=chosen_by, in0=pair_rows[:, 0:2 * TOK], scalar=code, in1=pair_rows[:, 2 * TOK:4 * TOK],
                                            op0=ALU.is_equal, op1=ALU.mult).then_inc(half_way, 1)
                    ve.wait_ge(half_way, count)
                    scaled(out, chosen_by[:, 0:TOK], chosen_by[:, TOK:2 * TOK], ALU.add).then_inc(ready, 1)

                def add(q, rounds, t=0):
                    for r in rounds:
                        ve.wait_ge(sem("spread_filled"), PAIR_ROUNDS * (UNROLL // 2) * t + (PAIR_ROUNDS * (NE // 2 * l + q) + r + 1))
                        two = banks[:, 4 + 2 * (r % 2):6 + 2 * (r % 2), 0:TOK]
                        scaled(moe_sum[:, 2 * r:2 * r + 2, :], moe_sum[:, 2 * r:2 * r + 2, :], two, ALU.add).then_inc(sem("spread_added"), 1)

                def step(n, t=0):
                    hidden(n, t)
                    if n < NE - 1:
                        rows_copy(n + 1, t)
                    if n % 2 == 0:
                        place_weights(n // 2 - 1, t)
                    if n >= 3:
                        add((n - 3) // 2, ((0, 1), (2, 3))[(n - 3) % 2], t)

                rows_copy(0)
                hidden(0)
                rows_copy(1)
                is_read(ve, ("codes", l, NT - 1))
                ve.wait_ge(sem("pair_codes_ready"), l + 1)
                ve.wait_ge(sem("moe_sum_cleared"), l + 1)
                for n in range(1, STEPS_AHEAD + 1):
                    step(n)
                with ve.Fori(0, BODIES) as t:
                    for n in range(STEPS_AHEAD + 1, STEPS_AHEAD + 1 + UNROLL):
                        step(n, t)
                for n in range(STEPS_AHEAD + 1 + UNROLL * BODIES, NE):
                    step(n)
                place_weights(NE // 2 - 1)
                add(NE // 2 - 2, (2, 3))
                add(NE // 2 - 1, (0, 1, 2, 3))
                ve.wait_ge(sem("spread_added"), PAIR_ROUNDS * NE // 2 * (l + 1))

                link(ve.tensor_scalar(further_code[:, :], row_of[:, :], float(NE * ROWS - ROWS), None, ALU.add))

                def further_turn(i):
                    ve.wait_ge(sem(f"further{l}_rows_turned"), i + 1)
                    ve.tensor_copy(teT[0].rearrange("p c r -> p (c r)"), bank[0][:, :]).then_inc(sem(f"further{l}_rowsT"), 1)
                    ve.tensor_scalar(further_code[:, :], further_code[:, :], float(ROWS), None, ALU.add).then_inc(sem(f"further{l}_code"), 1)
                    ve.wait_ge(sem(f"further{l}_code"), i + 1)
                    place(weights_at[0], further_code[:, 0:1], sem(f"further{l}_choices"), i + 1, sem(f"further{l}_weights"))
                    ve.wait_ge(sem(f"further{l}_weights"), i + 1)
                    ve.wait_ge(sem(f"further{l}_silu"), i + 1)
                    scaled(hid[:, 0, :], sgate[:, 0, :], bank[2][0:ROWS, 0:FF]).then_inc(sem(f"further{l}_hid"), 1)
                    ve.wait_ge(sem(f"further{l}_down"), i + 1)
                    ve.tensor_copy(y_further[:, 0:512], bank[4][0:ROWS, :])
                    ve.tensor_copy(y_further[:, 512:D], bank[5][0:ROWS, :]).then_inc(sem(f"further{l}_y"), 1)
                    for r in range(PAIR_ROUNDS):
                        ve.wait_ge(sem(f"further{l}_spread"), PAIR_ROUNDS * i + (r + 1))
                        scaled(moe_sum[:, 2 * r:2 * r + 2, :], moe_sum[:, 2 * r:2 * r + 2, :], banks[:, 6:8, 0:TOK],
                               ALU.add).then_inc(sem(f"further{l}_added"), 1)
                    ve.wait_ge(sem(f"further{l}_added"), PAIR_ROUNDS * i + PAIR_ROUNDS)

                further_turns(ve, l, further_turn)

            def final(t):
                is_filled(ve, ("final", t, 1))
                done(ve.tensor_copy(xout[:, t, 512:D], psum(("final", t, 1))))

            ve.memset(eps[:, :], EPS)
            ve.memset(prefix[:, :, :], 0.0)
            ve.memset(condS[:, :, :], 0.0)
            ve.memset(uT, 0.0).then_inc(sem("constants_ready_v"), 1)
            ve.wait_ge(sem("constants_ready_v"), 1)
            is_filled(ve, "vectors")
            done(ve.tensor_copy(cols[:, :], psum("vectors")[:, 0:NCOL]))
            is_read(ve, "vectors")
            ve.wait_ge(sem("constants_ready"), 1)
            link(ve.tensor_copy(turn_row[:, :], iota[:, :]))
            link(ve.tensor_copy(row_of[:, :], row_iota[:, :]))
            link(ve.tensor_scalar(ramp[:, :], turn_row[:, :], -1.0 / ROWS, float(NE), ALU.mult, ALU.add))
            normed(0, 0)
            for s in range(2):
                ada_columns(0, s)
            for l in range(DEPTH):
                if l:
                    normed(l, 0)
                taps = iter(())
                if l == 0:
                    ve.wait_ge(sem("rows_of_gains_loaded"), 16 * 14)
                    for a, n, f in ((B_QN, QK, QK ** -0.5), (B_DQN, DK, DK ** -0.5), (B_SUB, DV, 1.0 - LAMBDA_INIT)):
                        link(ve.tensor_scalar(bc[:, a:a + n], bc[:, a:a + n], f, None, ALU.mult))
                    for i in range(2):
                        a = B_LAM + 2 * DK * i
                        link(scaled(bc[:, a:a + DK], bc[:, a:a + DK], bc[:, a + DK:a + 2 * DK]))
                        ins = ve.tensor_reduce(out=lam[:, i:i + 1], in_=bc[:, a:a + DK], axis=AX.X, op=ALU.add)
                        if i == 0:
                            link(ins)
                        else:
                            ins.then_inc(sem("lambda_sums"), 1)
                    taps = conv_taps()
                    for i, (kind, js) in enumerate(IN_BLOCKS):
                        if kind == "glu_g":
                            for j in js:
                                is_read(ve, ("glu_g", j))
                                for a, b, dst in ((0, CTX, PADC), (CTX, TOK, 2 * PADC + CTX)):
                                    ins = scaled(uT[:, j, dst:dst + b - a], glu_a[:, j, a:b], glu_g[:, j, a:b])
                                    ins.then_inc(sem("u_ready"), 1)
                            ve.wait_ge(sem("u_ready"), 2 * js[1] + 2)
                        if i - 1 in ADA_AFTER_BLOCK:
                            ada_columns(*ADA_AFTER_BLOCK[i - 1])
                        for _ in range((0, 15, 16, 10, 10, 5, 0)[i]):
                            next(taps)
                    ve.wait_ge(sem("lambda_exps"), 1)
                    link(scaled(lam[:, 4:5], lam[:, 3:4], lam[:, 2:3], ALU.subtract))
                    link(ve.tensor_scalar(lam[:, 5:6], lam[:, 4:5], -LAMBDA_INIT, None, ALU.add))
                    ve.wait_ge(sem("u_ready"), 8)
                    ve.wait_ge(sem("latent_std"), 1)
                    link(ve.reciprocal(small[:, 7, 0:2 * NT], small[:, 7, 0:2 * NT]))
                    for t in range(NT):
                        ve.tensor_scalar(proj[:, t, 0:QR], proj[:, t, 0:QR], small[:, 7, 2 * t:2 * t + 1], None,
                                         ALU.mult).then_inc(sem("qa_normed"), 1)
                    for t in range(NT):
                        ve.scalar_tensor_tensor(out=ckv[:, t, :], in0=proj[:, t, QR:QR + KVR], scalar=small[:, 7, 2 * t + 1:2 * t + 2],
                                                in1=bc[:, B_KVN:B_KVN + KVR], op0=ALU.mult, op1=ALU.mult).then_inc(sem("ckv_normed"), 1)
                    ve.wait_ge(sem("pad_stored"), 16)
                    ve.wait_ge(sem("cache_loaded"), 32)
                    for t in range(4):
                        src = proj[:, t, QR + KVR:REST] if t < NT else krope_c
                        ve.tensor_copy(k_e[:, t, :, NOPE:], src.unsqueeze(1).to_broadcast((P, HEADS, ROPE))).then_inc(sem("k_rope_placed"), 1)
                    for j in range(2):
                        is_filled(ve, ("ckvT", j))
                        done(ve.tensor_copy(ckvT[:, j, :], psum(("ckvT", j))))
                    for b in range(2):
                        for t in range(NT):
                            is_filled(ve, ("q", b, t))
                            done(ve.tensor_copy(q_e[:, t, 384 * b:384 * b + 384], psum(("q", b, t))[:, 0:384]))
                    is_read(ve, ("q", 1, 2))
                    head_norm(0, a1[:, 0:NT * HEADS * QK].rearrange("p (r e) -> p r e", e=QK), NT * HEADS, QK, bc[:, B_QN:B_QN + QK], "heads_normed")
                    head_norm(1, a2[:, 0:4 * HEADS * QK].rearrange("p (r e) -> p r e", e=QK), 4 * HEADS, QK, bc[:, B_KN:B_KN + QK], "heads_normed")
                    ve.wait_ge(sem("cache_stored"), 32)
                else:
                    for b in range(12):
                        for t in range(NT):
                            if (b * NT + t) % 2:
                                is_filled(ve, ("qkv", b, t))
                                dst = (q_o, k_o, v_o)[b // 4]
                                done(ve.tensor_copy(dst[:, t, 256 * (b % 4):256 * (b % 4) + 256], psum(("qkv", b, t))[:, 0:256]))
                        if b in (4, 8):
                            buf, gain = ((a1[:, :], B_DQN), (a2[:, 0:3072], B_DKN))[b // 4 - 1]
                            is_read(ve, ("qkv", b - 1, 2))
                            is_read(ve, ("qkv", b - 1, 1))
                            head_norm(1 + b // 4, buf.rearrange("p (r e) -> p r e", e=DK), NT * 2 * HEADS, DK, bc[:, gain:gain + DK], "heads_normed")
                for h in range(HEADS):
                    is_filled(ve, ("kT", l, h))
                    n = QK if l == 0 else P
                    done(ve.tensor_copy(kT[0:n, h, :], psum(("kT", l, h))[0:n, :]))
                attention(l, taps)
                if l == 0:
                    ve.wait_ge(sem("vector_step"), step[0])
                    ve.nop().then_inc(sem("conv_ready"), 1)
                    is_filled(ve, "conv_mean")
                    for j in range(NCH):
                        ins = ve.scalar_tensor_tensor(out=conv_acc[:, j, :], in0=psum("conv_mean")[:, 0:CONVO], scalar=-1.0 / CH,
                                                      in1=conv_acc[:, j, :], op0=ALU.mult, op1=ALU.add)
                    done(ins)
                    is_read(ve, "conv_var")
                    link(ve.reciprocal(rstd[:, :], std[:, :]))
                    for j in range(NCH):
                        scaled(conv_acc[:, j, :], conv_acc[:, j, :], rstd[:, :]).then_inc(sem("conv_normed"), 1)
                else:
                    is_read(ve, ("o", 1, len(attention_units(1)) - 1))
                    head_norm(4, a7[:, 0:3072].rearrange("p (r e) -> p r e", e=DV), NT * HEADS, DV, bc[:, B_SUB:B_SUB + DV], "o_normed")
                mixer_residual(l)
                normed(l, 1)
                routing(l)
                experts(l)
                expert_residual(l)
            ve.wait_ge(sem("cache_stored"), 64)
            for t in range(NT):
                final(t)

        @block.gpsimd
        def _(pool):
            step = [0]

            def link(ins):
                step[0] += 1
                ins.then_inc(sem("pool_step"), 1)
                pool.wait_ge(sem("pool_step"), step[0])

            def rope(x1, x2, cos, sin, tmp, ready, count=0):
                a, b, c = tmp
                tt = pool.tensor_tensor
                tt(out=a, in0=x1, in1=sin, op=ALU.mult)
                tt(out=b, in0=x2, in1=cos, op=ALU.mult)
                link(tt(out=c, in0=x2, in1=sin, op=ALU.mult))
                link(tt(out=x1, in0=x1, in1=cos, op=ALU.mult))
                link(tt(out=x1, in0=x1, in1=c, op=ALU.subtract))
                ins = tt(out=x2, in0=a, in1=b, op=ALU.add)
                if ready:
                    ins.then_inc(sem(ready), 1)
                    pool.wait_ge(sem(ready), count)
                else:
                    link(ins)

            link(pool.memset(ident[:, :], 0.0))
            link(pool.memset(ones[:, :], 1.0))
            link(pool.affine_select(out=ident[:, :], in_=ident[:, :], compare_op=ALU.not_equal, fill=1.0, base=0,
                                    pattern=[[-1, P]], channel_multiplier=1))
            link(pool.affine_select(out=below[:, :], in_=ones[:, :], compare_op=ALU.is_gt, fill=0.0, base=0,
                                    pattern=[[1, P]], channel_multiplier=-1))
            link(pool.memset(pick[:, :, :], 0.0))
            for beyond in (0, 64):
                link(pool.affine_select(out=pick[:, :, :], in_=pick[:, :, :], compare_op=ALU.not_equal, fill=1.0, base=-beyond,
                                        pattern=[[-32, 2], [-1, 2]], channel_multiplier=1))
            link(pool.iota(row_iota[:, :], pattern=[[1, 1]], base=0, channel_multiplier=1))
            pool.iota(iota[:, :], pattern=[[ROWS, NE]], base=0, channel_multiplier=0).then_inc(sem("constants_ready"), 1)
            link(pool.memset(a2[0:ROWS, 0:D], 0.0))
            pool.dma_start(sorted_rows[PAIRS:PAIRS + ROWS, :], a2[0:ROWS, 0:D]).then_inc(sem("pad_stored"), 16)
            pool.wait_ge(sem("pad_stored"), 16)
            for v, k in ((qn_g[0], B_QN), (kn_g[0], B_KN), (dqn_g[0], B_DQN), (dkn_g[0], B_DKN), (sub_g[0], B_SUB),
                         (kvn_g[0], B_KVN), (lq1[0], B_LAM), (lk1[0], B_LAM + DK), (lq2[0], B_LAM + 2 * DK),
                         (lk2[0], B_LAM + 3 * DK), (moe_bg[0], B_MOE), (moe_be[0], B_MOE + NG),
                         (moe_bg[1], B_MOE + NG + NE), (moe_be[1], B_MOE + 2 * NG + NE)):
                pool.dma_start(bc[:, k:k + v.shape[0]], v.partition_broadcast(P)).then_inc(sem("rows_of_gains_loaded"), 16)
            pool.dma_start(rope16[:, :, :, :], rope_mla.rearrange("(t p) a n -> p t a n", p=P)).then_inc(sem("rope_loaded"), 16)
            pool.dma_start(rope32[:, :, :, :], rope_diff.rearrange("(t p) a n -> p t a n", p=P)).then_inc(sem("rope_loaded"), 16)
            for l in range(DEPTH):
                pool.dma_start(wr[:, l, :, 0:NG], moe_wg[l].rearrange("(k p) g -> p k g", p=P)).then_inc(sem("router_loaded"), 16)
                pool.dma_start(wr[:, l, :, NG:], moe_we[l].rearrange("(k p) g -> p k g", p=P)).then_inc(sem("router_loaded"), 16)

            def modulated(l, w):
                is_read(pool, ("adaT", l, 3 * w + 1))
                pool.wait_ge(sem("scales_ready"), 2 * l + w + 1)
                for c in range(KD):
                    pool.wait_ge(sem("hn_ready"), KD * (2 * l + w) + c + 1)
                    pool.tensor_scalar(hT[:, c, 0:CTX], hn[:, c, 0:CTX], mcol(l, 3 * w + 1, c, 0), mcol(l, 3 * w, c, 0),
                                       ALU.mult, ALU.add).then_inc(sem("h_ctx_ready"), 1)

            for l in range(DEPTH):
                modulated(l, 0)
                if l == 0:
                    pool.wait_ge(sem("rope_loaded"), 32)
                    is_read(pool, ("rest", 2, 0))
                    pool.wait_ge(sem("ckv_normed"), 1)
                    pool.dma_start(new_ckv[0, 0], ckv[:, 0, :]).then_inc(sem("cache_stored"), 16)
                    pool.dma_start(new_krope[0, 0], proj[:, 0, QR + KVR:REST]).then_inc(sem("cache_stored"), 16)
                    for i, (buf, ready) in enumerate(((a1, "q_ready"), (a2, "k_ready"))):
                        pool.wait_ge(sem("heads_normed"), i + 1)
                        x = buf[:, HEADS * QK:3 * HEADS * QK].rearrange("p (t h e) -> p t h e", t=2, h=HEADS)
                        half = ROPE // 2
                        cos, sin = (rope16[:, :, k, :].unsqueeze(2).to_broadcast((P, 2, HEADS, half)) for k in range(2))
                        tmp = [rope_tmp[:, k, 0:2 * HEADS * half].rearrange("p (t h e) -> p t h e", t=2, h=HEADS) for k in range(3)]
                        rope(x[:, :, :, NOPE:NOPE + half], x[:, :, :, NOPE + half:], cos, sin, tmp, ready, 1)
                else:
                    for i, (buf, ready) in enumerate(((q_o, "q_ready"), (k_o, "k_ready"))):
                        pool.wait_ge(sem("heads_normed"), i + 3)
                        if i == 1:
                            pool.dma_start(new_dk[0, 0].rearrange("p h m d -> p (h m d)"), k_o[:, 0, :]).then_inc(sem("cache_stored"), 16)
                        half = DK // 2
                        for t in (1, 2):
                            x = buf[:, t, :].rearrange("p (r e) -> p r e", e=DK)
                            cos, sin = (rope32[:, t - 1, k, :].unsqueeze(1).to_broadcast((P, 2 * HEADS, half)) for k in range(2))
                            tmp = [rope_tmp[:, k, :].rearrange("p (r e) -> p r e", e=half) for k in range(3)]
                            rope(x[:, :, 0:half], x[:, :, half:], cos, sin, tmp, ready if t == 2 else None, 2)
                    for b in (10, 11):
                        is_read(pool, ("qkv", b, 0))
                    pool.dma_start(new_dv[0, 0].rearrange("p h d -> p (h d)"), v_o[:, 0, :]).then_inc(sem("cache_stored"), 16)
                modulated(l, 1)
                is_read(pool, ("htok", l, NT - 1, 1))
                pool.memset(moe_sum[:, :, :], 0.0).then_inc(sem("moe_sum_cleared"), 1)
                pool.wait_ge(sem("places_ready"), l + 1)
                for k in range(2):
                    for t in range(NT):
                        pool.indirect_dma_start(out=sorted_rows, out_offset=bass.IndirectOffsetOnAxis(ap=idx_sorted[:, NT * k + t:NT * k + t + 1], axis=0),
                                                in_=htok[:, t, :], in_offset=None).then_inc(sem("rows_sorted"), 16)
            pool.wait_ge(sem("cache_stored"), 64)


def rope_tables(rot):
    quarter = rot // 4
    freqs = np.power(np.float32(10000.0), -np.arange(quarter, dtype=np.float32) / np.float32(quarter)).astype(np.float32)
    row = np.repeat(np.arange(LAT // 64, dtype=np.float32), 64)
    column = np.tile(np.arange(64, dtype=np.float32), LAT // 64)
    angle = np.concatenate([row[:, None] * freqs, column[:, None] * freqs], axis=-1)
    return np.stack([np.cos(angle), np.sin(angle)], axis=1).astype(np.float32)


_OUTS = [((1, 128, 1024), "float32"), ((1, 256, 1024), "float32"), ((1, 1, 128, 256), "float32"),
         ((1, 1, 128, 32), "float32"), ((1, 1, 128, 8, 2, 64), "float32"), ((1, 1, 128, 8, 128), "float32")]


def kernel(**inputs):
    import numpy as _np
    import concourse.bacc as _bacc
    from concourse import mybir as _mybir
    from concourse.bass_utils import run_bass_kernel_spmd as _run

    nc = _bacc.Bacc("TRN2", target_bir_lowering=False, num_devices=1)
    arrays, args = {}, []
    material = {name: inputs[name] for name in MATERIAL}
    material["rope_mla"], material["rope_diff"] = rope_tables(ROPE), rope_tables(DK)
    for name, a in material.items():
        a = _np.ascontiguousarray(a)
        arrays[f"in_{name}_dram"] = a
        args.append(nc.dram_tensor(f"in_{name}_dram", a.shape, _mybir.dt.from_np(a.dtype), kind="ExternalInput").ap())
    outs = [nc.dram_tensor(f"out_{i}_dram", shape, _mybir.dt.from_np(_np.dtype(dtype)), kind="ExternalOutput").ap()
            for i, (shape, dtype) in enumerate(_OUTS)]
    hybrid_trunk(nc, args[:-2], args[-2:], outs)
    r = _run(nc, [arrays], core_ids=[0])
    return tuple(r.results[0][f"out_{i}_dram"] for i in range(len(_OUTS)))
```

```python
import math
from contextlib import ExitStack

import numpy as np

import concourse.bass as bass
from concourse import mybir

ALU = mybir.AluOpType
ACT = mybir.ActivationFunctionType
AX = mybir.AxisListType
F32 = mybir.dt.float32
U32 = mybir.dt.uint32
I32 = mybir.dt.int32

P = 128
D = 1024
KD = D // P
DEPTH = 2
CTX, LAT = 128, 256
TOK = CTX + LAT
NT = TOK // P
EPS = 1e-6
CH, TAPS = 512, 31
NCH, PADC = CH // P, TAPS // 2
QR, KVR, ROPE, NOPE, HEADS = 384, 256, 32, 64, 8
QK = NOPE + ROPE
EVEN_IN = 2 * CH + QR + KVR + ROPE
REST = QR + KVR + ROPE
DK, DV = 64, 128
NG, EPG, NE, FF = 4, 8, 32, 256
ROWS = 64
ROUNDS = TOK // ROWS
PAIRS = 2 * TOK
RING = 6
BUFFERS = 2
UNROLL = 4
STEPS_AHEAD = 4
BODIES = (NE - 1 - STEPS_AHEAD) // UNROLL
PAIR_ROUNDS = KD // 2
SLOT = 2048
CONVW = PADC + CTX + PADC + LAT + PADC
CONVO = CTX + PADC + LAT
LAMBDA_INIT = 0.8 - 0.6 * math.exp(-0.3)
BIG = 1e30
SEG = ((0, CTX, 0), (CTX, TOK, 1))

B_QN, B_KN, B_DQN, B_DKN = 0, 96, 192, 256
B_SUB, B_KVN, B_LAM, B_MOE = 320, 448, 704, 960
NBC = B_MOE + DEPTH * (NG + NE)
M_WORK, M_EQ, M_SEL, M_SEL2, M_ONE1, M_ONE2, M_BOTH, M_PLACE, M_RANK = range(9)
(R_GMAX, R_GSUM, R_GATE, R_GTOP, R_M1, R_TOP1, R_M2, R_TOP2, R_D, R_ED, R_RANK1, R_RANK2, R_ID1, R_ID2,
 R_W1, R_W2, R_P1, R_P2, R_TURN) = range(19)
C_ADA, C_N1, C_N2 = 0, 96, 112
C_CW, C_CB = 128, 252
C_LNG, C_LNB, C_QRG, C_COND, C_CCTX, C_SUB = 256, 260, 264, 267, 275, 283
NCOL = 284

MATERIAL = ["x_prompt", "x_sample", "cache_mla_ckv", "cache_mla_krope", "cache_diff_k", "cache_diff_v",
            "c", "c_ctx", "ada_w", "ada_b", "norm1_g", "norm2_g", "ev_w_in", "ev_conv_w", "ev_conv_b",
            "ev_conv_ln_g", "ev_conv_ln_b", "ev_q_norm_g", "ev_w_qb", "ev_kv_norm_g", "ev_w_kvb",
            "ev_qn_g", "ev_kn_g", "ev_w_o", "od_w_qkv", "od_qn_g", "od_kn_g", "od_lambda_q1",
            "od_lambda_k1", "od_lambda_q2", "od_lambda_k2", "od_subln_g", "od_w_o", "moe_wg", "moe_bg",
            "moe_we", "moe_be", "moe_w_gate", "moe_w_up", "moe_w_down"]


FINAL_READERS = ("sss", "vsv")


class PsumGroups:

    def __init__(self, start=0):
        self.names, self.at, self.reader, self.count = [], {}, [], []
        self.read = {"v": 0, "s": 0}

    def add(self, name, reader):
        self.at[name] = len(self.names)
        self.names.append(name)
        self.reader.append(reader)
        self.read[reader] += 1
        self.count.append(self.read[reader])


def attention_units(l):
    return [(h, t, m) for h in range(HEADS) for t in range(NT) for m in range((1, 2)[l])]


IN_BLOCKS = [("glu_a", (0, 1)), ("glu_g", (0, 1)), ("glu_a", (2, 3)), ("glu_g", (2, 3)), ("rest", 0), ("rest", 1), ("rest", 2)]
ADA_AFTER_BLOCK = {1: (0, 2), 2: (0, 3), 3: (0, 4), 4: (0, 5), 5: (1, 0)}
ADA_AT_STEP = {2 + 5 * i: (1, 1 + i) for i in range(5)}
ADA_LAG = 3
CONV_AT_STEP = {"mean": 8, "centre": 8, "squares": 9, "var": 11, "std": 11, "normed": 12}


def attention_steps(l):
    n = len(attention_units(l))
    width, lag = ((1, 2), (2, 1))[l]
    for s in range(n // width + lag + 1):
        def units(behind):
            return [u for u in range(width * (s - behind), width * (s - behind) + width) if 0 <= u < n]
        yield (units(0), units(lag), units(lag + 1),
               ADA_AT_STEP.get(s) if l == 0 else None, ADA_AT_STEP.get(s - ADA_LAG) if l == 0 else None,
               [what for what, at in CONV_AT_STEP.items() if l == 0 and at == s])


def output_heads():
    steps = list(attention_steps(1))
    last_of = {(2 * NT * (h + 1) - 1): h for h in range(HEADS)}
    yield None
    for work in steps:
        yield next((last_of[u] for u in work[2] if u in last_of), None)


TURNED_READERS = ("sss", "ssv")


def psum_order():
    g = PsumGroups()
    g.add("vectors", "v")
    for c in range(KD):
        g.add(("xT", c), "s")
    g.add(("sumsq", 0, 0), "s")
    for s in range(2):
        g.add(("ada", 0, s), "s")
        g.add(("adaT", 0, s), "v")
    for l in range(DEPTH):
        if l == 0:
            for i, (kind, js) in enumerate(IN_BLOCKS):
                if kind == "rest":
                    for t in range(NT):
                        g.add(("rest", js, t), "s")
                else:
                    for j in js:
                        g.add((kind, j), "s")
                if i - 1 in ADA_AFTER_BLOCK:
                    g.add(("adaT",) + ADA_AFTER_BLOCK[i - 1], "v")
                if i in ADA_AFTER_BLOCK:
                    g.add(("ada",) + ADA_AFTER_BLOCK[i], "s")
            for j in range(3):
                g.add(("qanT", j), "s")
            for j in range(2):
                g.add(("ckvT", j), "v")
            for b in range(2):
                for t in range(NT):
                    g.add(("q", b, t), "v")
            for t in range(NT + 1):
                for b in range(2):
                    g.add(("kv", t, b), "s")
        else:
            g.add(("sumsq", l, 0), "s")
            for b in range(12):
                for t in range(NT):
                    g.add(("qkv", b, t), "sv"[(b * NT + t) % 2])
        for h in range(HEADS):
            g.add(("qT", l, h), "s")
        for h in range(HEADS):
            g.add(("kT", l, h), "v")
        for scores, turned, outs, sums, columns, conv in attention_steps(l):
            for u in scores:
                g.add(("S", l, u), "s")
            for u in turned:
                g.add(("pT", l, u), TURNED_READERS[l][u % 3])
            for u in outs:
                g.add(("o", l, u), "v")
            if sums:
                g.add(("ada",) + sums, "s")
            if columns:
                g.add(("adaT",) + columns, "v")
            if "mean" in conv:
                g.add("conv_mean", "v")
            if "var" in conv:
                g.add("conv_var", "s")
        for j in range((NCH, KD)[l]):
            g.add(("oT", l, j), "s")
        for c in range(KD):
            g.add(("out", l, c), "v")
        g.add(("sumsq", l, 1), "s")
        g.add(("router", l), "v")
        for t in range(NT):
            for b in range(2):
                g.add(("htok", l, t, b), "s")
        g.add(("rank", l), "v")
        for i in range(NT):
            g.add(("codes", l, i), "s")
        for i in range(PAIRS // P):
            for b in range(2):
                g.add(("sorted", l, i, b), "vs"[b])
        g.add(("first", l), "v")
    for b in range(2):
        for t in range(NT):
            g.add(("final", t, b), FINAL_READERS[b][t])
    return g


def weight_order():
    out = []

    def ada(l, s):
        for k in range(4):
            out.append((("ada", l, s, k), ("ada", l, s)))

    for l in range(DEPTH):
        if l == 0:
            ada(0, 0)
            for i, (kind, js) in enumerate(IN_BLOCKS):
                if kind == "rest":
                    out.append((("w_in", 4 + js), ("rest", js, 2)))
                else:
                    out.append((("w_in", js[0] // 2 + (0 if kind == "glu_a" else 2)), (kind, js[1])))
                if i in ADA_AFTER_BLOCK:
                    ada(*ADA_AFTER_BLOCK[i])
            for b in range(2):
                out.append((("w_qb", b), ("q", b, 2)))
            out.append((("w_kvb",), ("kv", 3, 1)))
            for s in sorted(ADA_AT_STEP):
                ada(*ADA_AT_STEP[s])
        else:
            for b in range(12):
                out.append((("w_qkv", b), ("qkv", b, 2)))
        for b in range(4):
            out.append((("w_o", l, b), ("out", l, 2 * b + 1)))
        out.append(("experts", l))
    return out


def hybrid_trunk(nc, ins, tables, outs):
    (x_prompt, x_sample, c_ckv, c_krope, c_dk, c_dv, c_vec, c_ctx, ada_w, ada_b, n1g, n2g, w_in, conv_w,
     conv_b, ln_g, ln_b, qr_g, w_qb, kvn_g, w_kvb, qn_g, kn_g, ev_wo, w_qkv, dqn_g, dkn_g, lq1, lk1, lq2,
     lk2, sub_g, od_wo, moe_wg, moe_bg, moe_we, moe_be, e_gate, e_up, e_down) = ins
    rope_mla, rope_diff = tables
    y_prompt, y_sample, new_ckv, new_krope, new_dk, new_dv = outs
    groups = psum_order()
    sorted_rows = nc.dram_tensor("sorted_rows", (PAIRS + ROWS, D), F32, kind="Internal").ap()

    with ExitStack() as ctx:
        def sb(name, shape, dt=F32):
            return ctx.enter_context(nc.sbuf_tensor(name, shape, dt))

        sems = {}

        def sem(name):
            if name not in sems:
                sems[name] = ctx.enter_context(nc.semaphore(name))
            return sems[name]

        banks = ctx.enter_context(nc.psum_tensor("banks", [P, 8, 512], F32))
        bank = [banks[:, i, :] for i in range(8)]

        ring = sb("ring", [P, RING, SLOT])
        xT = sb("xT", [P, KD, TOK])
        hT = sb("hT", [P, KD, TOK])
        a1 = sb("a1", [P, 3072])
        a23 = sb("a23", [P, 8192])
        a2, a3 = a23[:, 0:4096], a23[:, 4096:8192]
        a4 = sb("a4", [P, 3072])
        a5 = sb("a5", [P, 4096])
        a6 = sb("a6", [P, 3072])
        a7 = sb("a7", [P, 1536 + NCH * CONVW])
        wr = sb("wr", [P, DEPTH, KD, NG + NE])
        cols = sb("cols", [P, NCOL])
        bc = sb("bc", [P, NBC])
        mod = sb("mod", [P, DEPTH, 6, KD, 2])
        condS = sb("condS", [P, KD, 32])
        ada_rows = sb("ada_rows", [P, 512])
        pick = sb("pick", [P, 2, 2])
        ident = sb("ident", [P, P])
        ones = sb("ones", [P, P])
        below = sb("below", [P, P])
        ramp = sb("ramp", [P, NE])
        turn_row = sb("turn_row", [P, NE])
        rope16 = sb("rope16", [P, 2, 2, ROPE // 2])
        rope32 = sb("rope32", [P, 2, 2, DK // 2])
        eps = sb("eps", [P, 1])
        iota = sb("iota", [P, NE], I32)
        std = sb("std", [P, CONVO])
        rstd = sb("rstd", [P, CONVO])
        pbuf = sb("pbuf", [P, 4, TOK])
        pTbuf = sb("pTbuf", [P, 4, 3, P])
        small = sb("small", [P, 8, 64])
        negmax = sb("negmax", [P, 48])
        rowsum = sb("rowsum", [P, 48])
        rinv = sb("rinv", [P, 48])
        lam = sb("lam", [P, 8])
        rt = sb("rt", [P, 10, NT * NE])
        rs = sb("rs", [P, 20, NT])
        logits = sb("logits", [P, NT, NG + NE])
        prefix = sb("prefix", [P, 2, 16 + NE])
        idx_sorted = sb("idx_sorted", [P, 2 * NT], U32)
        row_of = sb("row_of", [P, 1])
        row_iota = sb("row_iota", [P, 1], I32)
        further_code = sb("further_code", [P, 1])
        starts = sb("starts", [P, ROUNDS * NE], I32)
        overflow = sb("overflow", [P, DEPTH], I32)
        sgate = a6[0:ROWS, 0:BUFFERS * FF].rearrange("p (b f) -> p b f", b=BUFFERS)
        hid = a6[0:ROWS, BUFFERS * FF:2 * BUFFERS * FF].rearrange("p (b f) -> p b f", b=BUFFERS)
        hidT = a6[:, 2 * BUFFERS * FF:2 * BUFFERS * FF + 2 * BUFFERS * ROWS].rearrange("p (b j r) -> p b j r", b=BUFFERS, j=2)

        beside_ring = [a23[:, SLOT * k:SLOT * k + SLOT] for k in range(4)]
        xtok = a1[:, :].rearrange("p (t d) -> p t d", t=NT)
        htok = xtok
        packs = a6[:, 0:3 * P].rearrange("p (a b) -> p a b", a=3)
        scratch = a6[:, :]
        hn = a6[:, :].rearrange("p (c t) -> p c t", c=KD)
        glu_a = a6[:, 0:NCH * TOK].rearrange("p (c t) -> p c t", c=NCH)
        glu_g = a6[:, NCH * TOK:2 * NCH * TOK].rearrange("p (c t) -> p c t", c=NCH)
        proj = a5[:, 0:NT * REST].rearrange("p (t n) -> p t n", t=NT)
        ckv = a5[:, NT * REST:NT * REST + 4 * KVR].rearrange("p (t n) -> p t n", t=4)
        krope_c = a5[:, NT * REST + 4 * KVR:NT * REST + 4 * KVR + ROPE]
        qanT = a4[:, 0:3 * TOK].rearrange("p (c t) -> p c t", c=3)
        ckvT = a4[:, 3 * TOK:3 * TOK + 2 * 512].rearrange("p (c t) -> p c t", c=2)
        q_e = a1[:, 0:NT * HEADS * QK].rearrange("p (t n) -> p t n", t=NT)
        k_e = a2[:, 0:4 * HEADS * QK].rearrange("p (t h e) -> p t h e", t=4, h=HEADS)
        v_e = a3[:, 0:4 * HEADS * NOPE].rearrange("p (t n) -> p t n", t=4)
        conv_acc = a3[:, 2048:2048 + NCH * CONVO].rearrange("p (c t) -> p c t", c=NCH)
        qT = a4[:, :].rearrange("p (h t) -> p h t", h=HEADS)
        kT = a5[:, :].rearrange("p (h t) -> p h t", h=HEADS)
        o_e = a7[:, 0:NT * CH].rearrange("p (t n) -> p t n", t=NT)
        uT = a7[:, NT * CH:NT * CH + NCH * CONVW].rearrange("p (c t) -> p c t", c=NCH)
        rope_tmp = a7[:, 0:3 * 512].rearrange("p (k n) -> p k n", k=3)
        q_o = a1[:, :].rearrange("p (t n) -> p t n", t=NT)
        k_o = a2[:, :].rearrange("p (t n) -> p t n", t=4)
        v_o = a3[:, :].rearrange("p (t n) -> p t n", t=4)
        o_o = a7[:, 0:NT * D].rearrange("p (t n) -> p t n", t=NT)
        sorted_in = [(a4, a5)[i // 3][:, i % 3 * D:(i % 3 + 1) * D] for i in range(PAIRS // P)]
        sortedT = a23[:, 0:KD * (PAIRS + ROWS)].rearrange("p (c r) -> p c r", c=KD)
        te_further = a4[0:ROWS, 0:D]
        teT = [a5[:, i * 512:(i + 1) * 512].rearrange("p (c r) -> p c r", c=KD) for i in range(BUFFERS)]
        y_pair = [a5[:, D + i * D:2 * D + i * D] for i in range(BUFFERS)]
        y_further = a5[0:ROWS, 3 * D:4 * D]
        spread = a6[:, 2 * BUFFERS * FF + 2 * BUFFERS * ROWS:2 * BUFFERS * FF + 2 * BUFFERS * ROWS + 2 * TOK + BUFFERS * TOK]
        chosen_by = spread[:, 0:2 * TOK]
        weights_at = [spread[:, 2 * TOK + i * TOK:3 * TOK + i * TOK] for i in range(BUFFERS)]
        diagonals = a7[:, 0:4 * TOK].rearrange("p (a q) -> p a q", q=P)
        pair_codes = a7[:, 4 * TOK:4 * TOK + NE // 2]
        pair_rows = a7[:, 4 * TOK + NE:8 * TOK + NE]
        xout = a2[:, 0:3072].rearrange("p (t d) -> p t d", t=NT)
        conv_sq = a6[:, 0:NCH * CONVO].rearrange("p (c t) -> p c t", c=NCH)
        gsub, gexp, geq, grank, gone, gpen = (rt[:, 9, NT * NG * i:NT * NG * i + NT * NG] for i in range(6))

        order = weight_order()
        piece_at, waits_of, base_of = {}, [], {}
        n = 0
        for item in order:
            if item[0] == "experts":
                base_of[item[1]] = n
                n += 3 * NE
            else:
                piece_at[item[0]] = n
                n += 1
        last_reader = {piece_at[i[0]]: i[1] for i in order if i[0] != "experts"}

        def slot(i):
            return ring[:, i % RING, :]

        def landed(i, turns=0):
            return 16 * (i // RING + 1) + 16 * turns

        def slot_sem(i):
            return sem(f"slot{i % RING}_landed")

        def piece(kind, *key):
            return piece_at[(kind,) + key]

        def expert_piece(l, n, k):
            return base_of[l] + 3 * n + k

        def is_read(eng, name):
            i = groups.at[name]
            eng.wait_ge(sem({"v": "read_by_vector", "s": "read_by_scalar"}[groups.reader[i]]), groups.count[i])

        def is_filled(eng, name):
            eng.wait_ge(sem("filled"), groups.at[name] + 1)

        def psum(name):
            return bank[groups.at[name] % 8][:, :]

        def mcol(l, s, c, j):
            return mod[:, l, s, c, j:j + 1]

        def col(i):
            return cols[:, i:i + 1]

        def further_turns(eng, l, turn, until=None):
            eng.wait_ge(sem("starts_ready"), l + 1)
            many = eng.value_load(overflow[0:1, l:l + 1], min_val=0, max_val=1)
            with eng.If(many > 0):
                with eng.Fori(0, (ROUNDS - 1) * NE) as i:
                    turn(i)
                if until:
                    eng.wait_ge(sem(until[0]), until[1])

        def tile(t):
            return slice(P * t, P * t + P)

        block = ctx.enter_context(nc.Block())

        @block.sync
        def _(sp):
            def load_piece(i, src, width):
                sp.dma_start(slot(i)[:, 0:width].rearrange("p (k n) -> p k n", k=src.shape[1]), src).then_inc(slot_sem(i), 16)

            def free(i):
                if i >= RING and i - RING in last_reader:
                    sp.wait_ge(sem("filled"), groups.at[last_reader[i - RING]] + 1)
                elif i >= RING:
                    sp.wait_ge(sem("down_filled"), NE)

            def source(name):
                if name[0] == "ada":
                    _, l, s, k = name
                    return ada_w[l, 256 * k:256 * k + 256, D * s:D * s + D].rearrange("(k p) n -> p k n", p=P)
                if name[0] == "w_in":
                    b = name[1]
                    return w_in[0, :, 256 * b:min(256 * b + 256, EVEN_IN)].rearrange("(k p) n -> p k n", p=P)
                if name[0] == "w_qb":
                    return w_qb[0, :, 384 * name[1]:384 * name[1] + 384].rearrange("(k p) n -> p k n", p=P)
                if name[0] == "w_kvb":
                    return w_kvb[0].rearrange("(k p) n -> p k n", p=P)
                if name[0] == "w_qkv":
                    return w_qkv[0, :, 256 * name[1]:256 * name[1] + 256].rearrange("(k p) n -> p k n", p=P)
                w = (ev_wo, od_wo)[name[1]]
                return w[0, :, 256 * name[2]:256 * name[2] + 256].rearrange("(k p) n -> p k n", p=P)

            def expert_loads(l):
                def weights(n, t, steady, which=(0, 1, 2)):
                    for k in which:
                        w, used = ((e_gate, "gate_up_filled"), (e_up, "gate_up_filled"), (e_down, "down_filled"))[k]
                        i = expert_piece(l, n, k)
                        if steady:
                            sp.wait_ge(sem(used), BUFFERS * t + (NE * l + n - 1))
                        else:
                            free(i)
                        e = bass.ds(BUFFERS * t + n, 1)
                        sp.dma_start(slot(i), w[l, e].rearrange("e (p k) n -> (e p) (k n)", p=P)).then_inc(slot_sem(i), 16)

                for n in range(BUFFERS):
                    weights(n, 0, False)
                sp.wait_ge(sem("rows_sorted"), 16 * 2 * NT * (l + 1))
                for i, rows in enumerate(sorted_in):
                    sp.dma_start(rows, sorted_rows[P * i:P * i + P, :]).then_inc(sem(f"sorted{i}_loaded"), 16)
                weights(BUFFERS, 0, True, (0, 1))
                with sp.Fori(0, (NE - 2 * BUFFERS) // BUFFERS) as t:
                    for n in range(BUFFERS + 1, 2 * BUFFERS + 1):
                        weights(n, t, True, (0, 1))
                        weights(n - 1, t, True, (2,))
                weights(NE - 1, 0, True, (0, 1))
                weights(NE - 2, 0, True, (2,))
                weights(NE - 1, 0, True, (2,))

                def loads(j, e, i):
                    first = sp.value_load(starts[0:1, bass.ds(i + NE, 1)], min_val=0, max_val=PAIRS)
                    loaded = sem(f"further{l}_loaded")
                    if not (isinstance(i, int) and i == 0):
                        sp.wait_ge(sem(f"further{l}_added"), PAIR_ROUNDS * i)
                    sp.dma_start(te_further, sorted_rows[bass.ds(first, ROWS), :]).then_inc(loaded, 16)
                    for k, w in enumerate((e_gate, e_up, e_down)):
                        sp.dma_start(ring[:, k, :], w[l, bass.ds(e, 1)].rearrange("e (p k) n -> (e p) (k n)", p=P)).then_inc(loaded, 16)

                sp.wait_ge(sem("starts_ready"), l + 1)
                many = sp.value_load(overflow[0:1, l:l + 1], min_val=0, max_val=1)
                with sp.If(many > 0):
                    sp.wait_ge(sem("spread_added"), PAIR_ROUNDS * NE // 2 * (l + 1))
                    loads(0, 0, 0)
                    with sp.Fori(1, NE) as e:
                        loads(0, e, e)
                    with sp.Fori(1, ROUNDS - 1) as j:
                        with sp.Fori(0, NE) as e:
                            loads(j, e, NE * j + e)
                    sp.wait_ge(sem(f"further{l}_added"), PAIR_ROUNDS * (ROUNDS - 1) * NE)

            def load(item):
                src = source(item[0])
                load_piece(piece_at[item[0]], src, src.shape[1] * src.shape[2])

            sp.dma_start(packs[0:96, 0, :], ada_b.rearrange("l (n p) -> (l n) p", p=P)).then_inc(sem("vectors_loaded"), 16)
            sp.dma_start(packs[96:112, 0, :], n1g.rearrange("l (n p) -> (l n) p", p=P)).then_inc(sem("vectors_loaded"), 16)
            sp.dma_start(packs[112:128, 0, :], n2g.rearrange("l (n p) -> (l n) p", p=P)).then_inc(sem("vectors_loaded"), 16)
            at = 0
            for v in (ln_g[0], ln_b[0], qr_g[0], c_vec[0], c_ctx, sub_g[0]):
                k = v.shape[0] // P
                sp.dma_start(packs[at:at + k, 2, :], v.rearrange("(n p) -> n p", p=P)).then_inc(sem("vectors_loaded"), 16)
                at += k
            sp.dma_start(packs[0:124, 1, :], conv_w[0].rearrange("t (n p) -> (t n) p", p=P)).then_inc(sem("vectors_loaded"), 16)
            sp.dma_start(packs[124:128, 1, :], conv_b[0].rearrange("(n p) -> n p", p=P)).then_inc(sem("vectors_loaded"), 16)

            for i, item in enumerate(order):
                if i == 4:
                    for k in range(4):
                        src = source(("ada", 0, 1, k))
                        sp.dma_start(beside_ring[k].rearrange("p (k n) -> p k n", k=2), src).then_inc(sem(f"beside{k}_landed"), 16)
                if item[0] == "experts":
                    expert_loads(item[1])
                else:
                    i = piece_at[item[0]]
                    free(i)
                    if item[0] == ("w_in", 4):
                        sp.wait_ge(sem("filled"), groups.at[("xT", KD - 1)] + 1)
                        sp.dma_start(ckv[:, 3, :], c_ckv[0, 0]).then_inc(sem("cache_loaded"), 16)
                        sp.dma_start(krope_c, c_krope[0, 0]).then_inc(sem("cache_loaded"), 16)
                    if item[0] == ("w_qkv", 4):
                        sp.wait_ge(sem("filled"), groups.at[("out", 0, 0)] + 1)
                        sp.dma_start(k_o[:, 3, :], c_dk[0, 0].rearrange("p h m d -> p (h m d)")).then_inc(sem("cache_loaded"), 16)
                        sp.dma_start(v_o[:, 3, :], c_dv[0, 0].rearrange("p h d -> p (h d)")).then_inc(sem("cache_loaded"), 16)
                    load(item)
            for b in range(2):
                for t in range(NT):
                    is_read(sp, ("final", t, b))
                    dst = y_prompt[0] if t == 0 else y_sample[0, P * (t - 1):P * t, :]
                    sp.dma_start(dst[:, 512 * b:512 * b + 512], xout[:, t, 512 * b:512 * b + 512]).then_inc(sem("y_stored"), 16)
            sp.wait_ge(sem("y_stored"), 16 * 2 * NT)

        @block.tensor
        def _(pe):
            at = [0]

            def opened(name):
                i = groups.at[name]
                assert i == at[0], (name, i, at[0])
                at[0] += 1
                if i >= 8:
                    is_read(pe, groups.names[i - 8])
                return psum(name)

            def product(out, pairs, last=False, ready=None):
                for k, (lhsT, rhs) in enumerate(pairs):
                    if ready:
                        ready(k)
                    mm = pe.matmul(out, lhsT, rhs, start=(k == 0), stop=(k == len(pairs) - 1))
                if last:
                    mm.then_inc(sem("filled"), 1)

            def turn(out, parts):
                column = 0
                for part in parts:
                    r, w = part.shape[0], part.shape[1]
                    mm = pe.transpose(out[0:w, column:column + r], part, ident[0:r, 0:r])
                    column += r
                mm.then_inc(sem("filled"), 1)

            def arrived(*name):
                if name[:3] == ("ada", 0, 1):
                    pe.wait_ge(sem(f"beside{name[3]}_landed"), 16)
                    return beside_ring[name[3]]
                i = piece_at[name]
                pe.wait_ge(slot_sem(i), landed(i))
                return slot(i)

            def chunk_of_h(use):
                def ready(k):
                    pe.wait_ge(sem("h_lat_ready"), KD * use + k + 1)
                    pe.wait_ge(sem("h_ctx_ready"), KD * use + k + 1)
                return ready

            def ada_sums(l, s):
                out = opened(("ada", l, s))
                for k in range(0, KD, 2):
                    w = arrived("ada", l, s, k // 2).rearrange("p (k n) -> p k n", k=2)
                    for odd in range(2):
                        for half in range(2):
                            q = 32 * (2 * odd + half)
                            mm = pe.matmul(out[q:q + 32, :], condS[:, k + odd, :], w[:, odd, 512 * half:512 * half + 512],
                                           start=(k == 0), stop=(k == KD - 2), tile_position=(0, q))
                mm.then_inc(sem("filled"), 1)

            def ada_columns(l, s):
                out = opened(("adaT", l, s))
                is_read(pe, ("ada", l, s))
                for n in range(KD):
                    mm = pe.matmul(out[:, 2 * n:2 * n + 2], ada_rows[:, P * (n % 4):P * (n % 4) + P], pick[:, n // 4, :],
                                   start=True, stop=True)
                mm.then_inc(sem("filled"), 1)

            def sum_of_squares(l, w):
                out = opened(("sumsq", l, w))
                for c in range(KD):
                    pe.wait_ge(sem("squares_ready"), KD * (2 * l + w) + c + 1)
                    mm = pe.matmul(out[:, 0:TOK], ones[:, :], scratch[:, c * TOK:c * TOK + TOK],
                                   start=(c == 0), stop=(c == KD - 1))
                mm.then_inc(sem("filled"), 1)

            def even_projections():
                for i, (kind, js) in enumerate(IN_BLOCKS):
                    if kind == "rest":
                        width = min(256, REST - 256 * js)
                        w = arrived("w_in", 4 + js)[:, 0:KD * width].rearrange("p (k n) -> p k n", k=KD)
                        for t in range(NT):
                            product(opened(("rest", js, t))[:, 0:width],
                                    [(hT[:, k, tile(t)], w[:, k, :]) for k in range(KD)], True)
                    else:
                        w = arrived("w_in", js[0] // 2 + (0 if kind == "glu_a" else 2)).rearrange("p (k n) -> p k n", k=KD)
                        for j in js:
                            product(opened((kind, j))[:, 0:TOK],
                                    [(w[:, k, P * (j % 2):P * (j % 2) + P], hT[:, k, :]) for k in range(KD)], True,
                                    chunk_of_h(0) if i == 0 and j == 0 else None)
                    if i - 1 in ADA_AFTER_BLOCK:
                        ada_columns(*ADA_AFTER_BLOCK[i - 1])
                    if i in ADA_AFTER_BLOCK:
                        ada_sums(*ADA_AFTER_BLOCK[i])
                pe.wait_ge(sem("qa_normed"), NT)
                for j in range(3):
                    turn(opened(("qanT", j)), [proj[:, t, P * j:P * j + P] for t in range(NT)])
                pe.wait_ge(sem("ckv_normed"), NT)
                pe.wait_ge(sem("cache_loaded"), 32)
                for j in range(2):
                    turn(opened(("ckvT", j)), [ckv[:, t, P * j:P * j + P] for t in range(4)])
                is_read(pe, ("qanT", 2))
                for b in range(2):
                    w = arrived("w_qb", b)[:, 0:3 * 384].rearrange("p (k n) -> p k n", k=3)
                    for t in range(NT):
                        product(opened(("q", b, t))[:, 0:384],
                                [(qanT[:, k, tile(t)], w[:, k, :]) for k in range(3)], True)
                is_read(pe, ("ckvT", 1))
                w = arrived("w_kvb").rearrange("p (k n) -> p k n", k=2)
                for t in range(NT + 1):
                    for b in range(2):
                        product(opened(("kv", t, b)), [(ckvT[:, k, tile(t)], w[:, k, 512 * b:512 * b + 512]) for k in range(2)], True)

            def odd_projections():
                for b in range(12):
                    w = arrived("w_qkv", b).rearrange("p (k n) -> p k n", k=KD)
                    for t in range(NT):
                        product(opened(("qkv", b, t))[:, 0:256],
                                [(hT[:, k, tile(t)], w[:, k, :]) for k in range(KD)], True,
                                chunk_of_h(2) if b == 0 and t == 0 else None)

            def turned_heads(l):
                pe.wait_ge(sem("q_ready"), l + 1)
                for h in range(HEADS):
                    src = q_e[:, :, QK * h:QK * h + QK] if l == 0 else q_o[:, :, P * h:P * h + P]
                    turn(opened(("qT", l, h)), [src[:, t, :] for t in range(NT)])
                pe.wait_ge(sem("k_ready"), l + 1)
                pe.wait_ge(sem("k_normed"), NT + 1)
                if l == 1:
                    pe.wait_ge(sem("cache_loaded"), 64)
                for h in range(HEADS):
                    src = k_e[:, :, h, :] if l == 0 else k_o[:, :, P * h:P * h + P]
                    turn(opened(("kT", l, h)), [src[:, t, :] for t in range(4)])

            def attention(l):
                units = attention_units(l)
                is_read(pe, ("qT", l, HEADS - 1))
                is_read(pe, ("kT", l, HEADS - 1))
                for scores, turned, outs, sums, columns, conv in attention_steps(l):
                    for u in scores:
                        h, t, m = units[u]
                        out = opened(("S", l, u))
                        part = slice(0, QK) if l == 0 else slice(DK * m, DK * m + DK)
                        keys = slice(0, P) if t == 0 else slice(P, 4 * P)
                        n = keys.stop - keys.start
                        product(out[:, 0:n], [(qT[part, h, tile(t)], kT[part, h, keys])], True)
                    for u in turned:
                        n = 1 if units[u][1] == 0 else 3
                        out = opened(("pT", l, u))
                        is_read(pe, ("S", l, u))
                        turn(out, [pbuf[:, u % 4, tile(j)] for j in range(n)])
                    for u in outs:
                        h, t, m = units[u]
                        tiles = [0] if t == 0 else [1, 2, 3]
                        out = opened(("o", l, u))
                        is_read(pe, ("pT", l, u))
                        v = v_e if l == 0 else v_o
                        w = NOPE if l == 0 else DV
                        product(out[:, 0:w], [(pTbuf[:, u % 4, j, :], v[:, s, w * h:w * h + w]) for j, s in enumerate(tiles)], True)
                    if sums:
                        ada_sums(*sums)
                    if columns:
                        ada_columns(*columns)
                    if "mean" in conv:
                        out = opened("conv_mean")
                        pe.wait_ge(sem("conv_ready"), 1)
                        product(out[:, 0:CONVO], [(ones[:, :], conv_acc[:, j, :]) for j in range(NCH)], True)
                    if "var" in conv:
                        out = opened("conv_var")
                        pe.wait_ge(sem("conv_squares"), NCH)
                        product(out[:, 0:CONVO], [(ones[:, :], conv_sq[:, j, :]) for j in range(NCH)], True)

            def mixer_out(l):
                order = [4, 5, 6, 7, 0, 1, 2, 3] if l == 0 else list(range(KD))

                def mixed(k):
                    c = order[k]
                    if l == 0 and c < NCH:
                        pe.wait_ge(sem("conv_out"), 2 * c + 2)
                    else:
                        is_read(pe, ("oT", l, c - NCH if l == 0 else c))

                if l == 0:
                    is_read(pe, ("o", l, NT * HEADS - 1))
                    for j in range(NCH):
                        turn(opened(("oT", l, j)), [o_e[:, t, P * j:P * j + P] for t in range(NT)])
                else:
                    for j in range(KD):
                        pe.wait_ge(sem("o_normed"), j + 1)
                        turn(opened(("oT", l, j)), [o_o[:, t, P * j:P * j + P] for t in range(NT)])
                for b in range(4):
                    w = arrived("w_o", l, b).rearrange("p (k n) -> p k n", k=KD)
                    for c in range(2):
                        product(opened(("out", l, 2 * b + c))[:, 0:TOK],
                                [(w[:, k, P * c:P * c + P], hT[:, k, :]) for k in order], True,
                                mixed if b == 0 and c == 0 else None)

            def routing(l):
                out = opened(("router", l))
                pe.wait_ge(sem("router_loaded"), 64)
                for t in range(NT):
                    product(out[:, (NG + NE) * t:(NG + NE) * (t + 1)],
                            [(hT[:, k, tile(t)], wr[:, l, k, :]) for k in range(KD)], t == NT - 1,
                            chunk_of_h(2 * l + 1) if t == 0 else None)
                for t in range(NT):
                    for b in range(2):
                        turn(opened(("htok", l, t, b)), [hT[:, 4 * b + j, tile(t)] for j in range(4)])
                out = opened(("rank", l))
                pe.wait_ge(sem("chosen"), l + 1)
                m = rt[:, M_BOTH, :].rearrange("p (t e) -> p t e", t=NT)
                for t in range(NT):
                    product(out[:, NE * t:NE * t + NE], [(ones[:, :], m[:, s, :]) for s in range(t)] + [(below[:, :], m[:, t, :])])
                product(out[:, NE * NT:NE * NT + NE], [(ones[:, :], m[:, s, :]) for s in range(NT)], True)
                pe.wait_ge(sem("diagonals_ready"), l + 1)
                for i in range(NT):
                    product(opened(("codes", l, i)), [(ones[:, :], diagonals[:, 4 * i:4 * i + 4, :])], True)
                for i in range(PAIRS // P):
                    pe.wait_ge(sem(f"sorted{i}_loaded"), 16 * (l + 1))
                    for b in range(2):
                        turn(opened(("sorted", l, i, b)), [sorted_in[i][:, c:D:KD] for c in range(4 * b, 4 * b + 4)])
                    if i == PAIRS // P - 1:
                        out = opened(("first", l))
                        w = []
                        for k in range(2):
                            j = expert_piece(l, 0, k)
                            pe.wait_ge(slot_sem(j), landed(j))
                            w.append(slot(j).rearrange("p (k n) -> p k n", k=KD))
                        for c in range(KD):
                            for k in range(2):
                                mm = pe.matmul(out[ROWS * k:ROWS * k + ROWS, 0:FF], sortedT[:, c, 0:ROWS], w[k][:, c, :],
                                               start=(c == 0), stop=(c == KD - 1), tile_position=(0, ROWS * k))
                        mm.then_inc(sem("filled"), 1)
                        is_filled(pe, ("first", l))
                        pe.nop().then_inc(sem("gate_up_filled"), 1)

            def experts(l):
                base = NE * l

                def gate_up(n, t=0):
                    w = []
                    for k in range(2):
                        i = expert_piece(l, n, k)
                        pe.wait_ge(slot_sem(i), landed(i) + 16 * (UNROLL // BUFFERS) * t)
                        w.append(slot(i).rearrange("p (k n) -> p k n", k=KD))
                    pe.wait_ge(sem("rowsT_ready"), UNROLL * t + (base + n + 1))
                    if base + n:
                        pe.wait_ge(sem("hid_ready"), UNROLL * t + (base + n))
                    for c in range(KD):
                        for k in range(2):
                            mm = pe.matmul(bank[1][ROWS * k:ROWS * k + ROWS, 0:FF], teT[n % BUFFERS][:, c, :], w[k][:, c, :],
                                           start=(c == 0), stop=(c == KD - 1), tile_position=(0, ROWS * k))
                    mm.then_inc(sem("gate_up_filled"), 1)

                def await_hid(n, t=0):
                    pe.wait_ge(sem("hid_ready"), UNROLL * t + (base + n + 1))
                    if base + n:
                        pe.wait_ge(sem("hidT_ready"), UNROLL * t + (base + n))

                def hid_turn(n):
                    for j in range(2):
                        mm = pe.transpose(bank[2][:, ROWS * j:ROWS * j + ROWS], hid[:, n % BUFFERS, j:FF:2], ident[0:ROWS, 0:ROWS])
                    mm.then_inc(sem("hid_turned"), 1)

                def down(n, t=0):
                    i = expert_piece(l, n, 2)
                    pe.wait_ge(slot_sem(i), landed(i) + 16 * (UNROLL // BUFFERS) * t)
                    pe.wait_ge(sem("hidT_ready"), UNROLL * t + (base + n + 1))
                    if base + n:
                        pe.wait_ge(sem("y_copied"), UNROLL * t + (base + n))
                    for j in range(2):
                        for b in range(2):
                            mm = pe.matmul(bank[3][ROWS * b:ROWS * b + ROWS, :], hidT[:, n % BUFFERS, j, :],
                                           slot(i)[:, D * j + 512 * b:D * j + 512 * b + 512], start=(j == 0), stop=(j == 1),
                                           tile_position=(0, ROWS * b))
                    mm.then_inc(sem("down_filled"), 1)

                def spread_out(q, rounds, t=0):
                    q_all, bodies = NE // 2 * l + q, UNROLL // 2 * t
                    if rounds[0] == 0:
                        pe.wait_ge(sem("y_copied"), UNROLL * t + (2 * q_all + 2))
                        pe.wait_ge(sem("weights_placed"), bodies + (q_all + 1))
                    for r in rounds:
                        if PAIR_ROUNDS * q_all + r > 1:
                            pe.wait_ge(sem("spread_added"), PAIR_ROUNDS * bodies + (PAIR_ROUNDS * q_all + r - 1))
                        for i in range(2):
                            mm = pe.matmul(bank[4 + 2 * (r % 2) + i][:, 0:TOK], y_pair[q % BUFFERS][:, P * (2 * r + i):P * (2 * r + i + 1)],
                                           weights_at[q % BUFFERS], start=True, stop=True)
                        mm.then_inc(sem("spread_filled"), 1)

                def step(n, t=0):
                    await_hid(n - 1, t)
                    gate_up(n, t)
                    hid_turn(n - 1)
                    if n >= 3:
                        spread_out((n - 3) // 2, ((0, 1), (2, 3))[(n - 3) % 2], t)
                    down(n - 1, t)

                for name in groups.names[at[0] - 8:at[0]]:
                    is_read(pe, name)
                for n in range(1, STEPS_AHEAD + 1):
                    step(n)
                with pe.Fori(0, BODIES) as t:
                    for n in range(STEPS_AHEAD + 1, STEPS_AHEAD + 1 + UNROLL):
                        step(n, t)
                for n in range(STEPS_AHEAD + 1 + UNROLL * BODIES, NE):
                    step(n)
                await_hid(NE - 1)
                hid_turn(NE - 1)
                spread_out(NE // 2 - 2, (2, 3))
                down(NE - 1)
                spread_out(NE // 2 - 1, (0, 1, 2, 3))
                pe.wait_ge(sem("spread_added"), PAIR_ROUNDS * NE // 2 * (l + 1))

                def further_turn(i):
                    pe.wait_ge(sem(f"further{l}_loaded"), 64 * i + 64)
                    for c in range(KD):
                        mm = pe.matmul(bank[0][:, ROWS * c:ROWS * c + ROWS], te_further[:, c:D:KD], ident[0:ROWS, 0:ROWS], start=True, stop=True)
                    mm.then_inc(sem(f"further{l}_rows_turned"), 1)
                    pe.wait_ge(sem(f"further{l}_rowsT"), i + 1)
                    for k in range(2):
                        w = ring[:, k, :].rearrange("p (k n) -> p k n", k=KD)
                        for c in range(KD):
                            mm = pe.matmul(bank[1 + k][0:ROWS, 0:FF], teT[0][:, c, :], w[:, c, :], start=(c == 0), stop=(c == KD - 1))
                    mm.then_inc(sem(f"further{l}_up"), 1)
                    pe.wait_ge(sem(f"further{l}_hid"), i + 1)
                    for j in range(2):
                        mm = pe.matmul(bank[3][:, ROWS * j:ROWS * j + ROWS], hid[:, 0, j:FF:2], ident[0:ROWS, 0:ROWS], start=True, stop=True)
                    mm.then_inc(sem(f"further{l}_hid_turned"), 1)
                    pe.wait_ge(sem(f"further{l}_hidT"), i + 1)
                    for b in range(2):
                        for j in range(2):
                            mm = pe.matmul(bank[4 + b][0:ROWS, :], hidT[:, 0, j, :], ring[:, 2, D * j + 512 * b:D * j + 512 * b + 512],
                                           start=(j == 0), stop=(j == 1))
                    mm.then_inc(sem(f"further{l}_down"), 1)
                    pe.wait_ge(sem(f"further{l}_y"), i + 1)
                    for r in range(PAIR_ROUNDS):
                        if r:
                            pe.wait_ge(sem(f"further{l}_added"), PAIR_ROUNDS * i + r)
                        for k in range(2):
                            mm = pe.matmul(bank[6 + k][:, 0:TOK], y_further[:, P * (2 * r + k):P * (2 * r + k + 1)],
                                           weights_at[0][0:ROWS, :], start=True, stop=True)
                        mm.then_inc(sem(f"further{l}_spread"), 1)

                further_turns(pe, l, further_turn, (f"further{l}_added", PAIR_ROUNDS * (ROUNDS - 1) * NE))

            def final():
                for b in range(2):
                    pe.wait_ge(sem("spread_added"), PAIR_ROUNDS * NE // 2 * DEPTH - PAIR_ROUNDS + PAIR_ROUNDS // 2 * (b + 1))
                    for t in range(NT):
                        turn(opened(("final", t, b)), [xT[:, 4 * b + j, tile(t)] for j in range(4)])

            pe.wait_ge(sem("constants_ready"), 1)
            pe.wait_ge(sem("vectors_loaded"), 16 * 11)
            turn(opened("vectors"), [packs[:, i, :] if i < 2 else packs[0:NCOL - 2 * P, 2, :] for i in range(3)])
            pe.wait_ge(sem("x_loaded"), 48)
            for c in range(KD):
                turn(opened(("xT", c)), [xtok[:, t, P * c:P * c + P] for t in range(NT)])
            sum_of_squares(0, 0)
            pe.wait_ge(sem("cond_ready"), 1)
            for s in range(2):
                ada_sums(0, s)
                ada_columns(0, s)
            for l in range(DEPTH):
                if l == 0:
                    even_projections()
                else:
                    sum_of_squares(l, 0)
                    odd_projections()
                turned_heads(l)
                attention(l)
                mixer_out(l)
                sum_of_squares(l, 1)
                routing(l)
                experts(l)
            final()

        @block.scalar
        def _(act):
            step = [0]

            def mark(ins):
                step[0] += 1
                ins.then_inc(sem("scalar_step"), 1)

            def done(ins):
                ins.then_inc(sem("read_by_scalar"), 1)

            def squares(l, w):
                for c in range(KD):
                    if l or w:
                        if w == 0:
                            act.wait_ge(sem("spread_added"), PAIR_ROUNDS * NE // 2 * l - PAIR_ROUNDS + c // 2 + 1)
                        else:
                            is_read(act, ("out", l, c))
                    act.activation(scratch[:, c * TOK:c * TOK + TOK], xT[:, c, :], ACT.Square).then_inc(sem("squares_ready"), 1)

            def modulated(l, w):
                is_filled(act, ("sumsq", l, w))
                done(act.activation(std[:, 0:TOK], psum(("sumsq", l, w))[:, 0:TOK], ACT.Sqrt, scale=1.0 / D, bias=eps[:, 0:1]))
                if l == 0 and w == 0:
                    for s in range(2):
                        ada_copy(0, s)
                is_read(act, ("adaT", l, 3 * w + 1))
                act.wait_ge(sem("scales_ready"), 2 * l + w + 1)
                for c in range(KD):
                    act.wait_ge(sem("hn_ready"), KD * (2 * l + w) + c + 1)
                    act.activation(hT[:, c, CTX:], hn[:, c, CTX:], ACT.Identity, scale=mcol(l, 3 * w + 1, c, 1),
                                   bias=mcol(l, 3 * w, c, 1)).then_inc(sem("h_lat_ready"), 1)

            def ada_copy(l, s):
                is_filled(act, ("ada", l, s))
                if (l, s) != (0, 0):
                    is_filled(act, ("adaT", l, s - 1) if s else ("adaT", 0, 5))
                done(act.activation(ada_rows[:, :], psum(("ada", l, s)), ACT.Copy))

            def head_std(l, i, buf, rows, width, view=None):
                act.activation(scratch[:, 0:rows * width], buf, ACT.Square).then_inc(sem("head_squares"), 1)
                act.wait_ge(sem("head_sums"), i + 1)
                act.activation(small[:, 2 * (i % 4) + 1, 0:rows], small[:, 2 * (i % 4), 0:rows], ACT.Sqrt,
                               scale=1.0 / width, bias=eps[:, 0:1]).then_inc(sem("head_stds"), 1)

            def output_squares(h):
                if h is not None:
                    is_read(act, ("o", 1, 2 * NT * (h + 1) - 1))
                    for t in range(NT):
                        k = NT * h + t
                        mark(act.activation(scratch[:, P * k:P * k + P], o_o[:, t, DV * h:DV * h + DV], ACT.Square, scale=DV ** -0.5,
                                            accum_out=small[:, 0, k:k + 1]))

            def experts(l):
                base = NE * l

                def silu(n, t=0):
                    act.wait_ge(sem("gate_up_filled"), UNROLL * t + (base + n + 1))
                    if base + n >= BUFFERS:
                        act.wait_ge(sem("hid_ready"), UNROLL * t + (base + n - 1))
                    gate = psum(("first", l)) if n == 0 else bank[1]
                    act.activation(sgate[:, n % BUFFERS, :], gate[0:ROWS, 0:FF], ACT.Silu).then_inc(sem("silu_done"), 1)

                def hid_copy(n, t=0):
                    act.wait_ge(sem("hid_turned"), UNROLL * t + (base + n + 1))
                    act.activation(hidT[:, n % BUFFERS, :, :].rearrange("p j r -> p (j r)"), bank[2][:, 0:2 * ROWS],
                                   ACT.Copy).then_inc(sem("hidT_ready"), 1)

                def y_copy(n, t=0):
                    act.wait_ge(sem("down_filled"), UNROLL * t + (base + n + 1))
                    before = NE // 2 * l + n // 2 - 1
                    if before > 0:
                        act.wait_ge(sem("spread_filled"), PAIR_ROUNDS * (UNROLL // 2) * t + PAIR_ROUNDS * before)
                    rows = slice(ROWS * (n % 2), ROWS * (n % 2) + ROWS)
                    act.activation(y_pair[n // 2 % BUFFERS][rows, 0:512], bank[3][0:ROWS, :], ACT.Copy)
                    act.activation(y_pair[n // 2 % BUFFERS][rows, 512:D], bank[3][ROWS:2 * ROWS, :], ACT.Copy).then_inc(sem("y_copied"), 1)

                def step(n, t=0):
                    silu(n, t)
                    hid_copy(n - 1, t)
                    y_copy(n - 1, t)

                act.wait_ge(sem("cache_stored"), 32 * (l + 1))
                for i in range(PAIRS // P):
                    is_filled(act, ("sorted", l, i, 1))
                    done(act.activation(sortedT[:, 4:8, P * i:P * i + P], psum(("sorted", l, i, 1)).rearrange("p (c r) -> p c r", c=4), ACT.Copy))
                silu(0)
                for n in range(1, STEPS_AHEAD + 1):
                    step(n)
                with act.Fori(0, BODIES) as t:
                    for n in range(STEPS_AHEAD + 1, STEPS_AHEAD + 1 + UNROLL):
                        step(n, t)
                for n in range(STEPS_AHEAD + 1 + UNROLL * BODIES, NE):
                    step(n)
                hid_copy(NE - 1)
                y_copy(NE - 1)

                def further_turn(i):
                    act.wait_ge(sem(f"further{l}_up"), i + 1)
                    act.activation(sgate[:, 0, :], bank[1][0:ROWS, 0:FF], ACT.Silu).then_inc(sem(f"further{l}_silu"), 1)
                    act.wait_ge(sem(f"further{l}_hid_turned"), i + 1)
                    act.activation(hidT[:, 0, :, :].rearrange("p j r -> p (j r)"), bank[3][:, 0:2 * ROWS],
                                   ACT.Copy).then_inc(sem(f"further{l}_hidT"), 1)

                further_turns(act, l, further_turn, (f"further{l}_added", PAIR_ROUNDS * (ROUNDS - 1) * NE))

            act.dma_start(xtok[:, 0, :], x_prompt[0]).then_inc(sem("x_loaded"), 16)
            for t in range(2):
                act.dma_start(xtok[:, 1 + t, :], x_sample[0, P * t:P * t + P, :]).then_inc(sem("x_loaded"), 16)
            is_read(act, "vectors")
            act.wait_ge(sem("constants_ready_v"), 1)
            for j, at in ((0, C_CCTX), (1, C_COND)):
                ins = act.activation(condS[:, :, j], cols[:, at:at + KD], ACT.Silu)
            ins.then_inc(sem("cond_ready"), 1)
            for c in range(KD):
                is_filled(act, ("xT", c))
                done(act.activation(xT[:, c, :], psum(("xT", c))[:, 0:TOK], ACT.Copy))
            act.wait_ge(sem("read_by_scalar"), groups.count[groups.at[("xT", KD - 1)]])
            for l in range(DEPTH):
                squares(l, 0)
                modulated(l, 0)
                if l == 0:
                    act.wait_ge(sem("lambda_sums"), 1)
                    act.activation(lam[:, 2:4], lam[:, 0:2], ACT.Exp).then_inc(sem("lambda_exps"), 1)
                    for i, (kind, js) in enumerate(IN_BLOCKS):
                        if kind == "rest":
                            width = min(256, REST - 256 * js)
                            for t in range(NT):
                                is_filled(act, ("rest", js, t))
                                done(act.activation(proj[:, t, 256 * js:256 * js + width], psum(("rest", js, t))[:, 0:width], ACT.Copy))
                            if js:
                                if js == 1:
                                    act.wait_ge(sem("u_ready"), 2 * NCH)
                                act.wait_ge(sem("read_by_scalar"), groups.count[groups.at[("rest", js, 2)]])
                                a, n = ((0, QR), (QR, KVR))[js - 1]
                                for t in range(NT):
                                    k = NT * (js - 1) + t
                                    mark(act.activation(scratch[:, QR * k:QR * k + n], proj[:, t, a:a + n], ACT.Square, scale=float(n) ** -0.5,
                                                        accum_out=small[:, 6, 2 * t + js - 1:2 * t + js]))
                        else:
                            for j in js:
                                is_filled(act, (kind, j))
                                dst, f = (glu_a, ACT.Copy) if kind == "glu_a" else (glu_g, ACT.Sigmoid)
                                done(act.activation(dst[:, j, :], psum((kind, j))[:, 0:TOK], f))
                        if i in ADA_AFTER_BLOCK:
                            ada_copy(*ADA_AFTER_BLOCK[i])
                    act.wait_ge(sem("scalar_step"), step[0])
                    act.activation(small[:, 7, 0:2 * NT], small[:, 6, 0:2 * NT], ACT.Sqrt, bias=eps[:, 0:1]).then_inc(sem("latent_std"), 1)
                    for j in range(3):
                        is_filled(act, ("qanT", j))
                        done(act.activation(qanT[:, j, :], psum(("qanT", j))[:, 0:TOK], ACT.Identity, scale=col(C_QRG + j)))
                    is_read(act, ("q", 1, 2))
                    head_std(l, 0, q_e.rearrange("p t n -> p (t n)"), NT * HEADS, QK)
                    act.wait_ge(sem("pad_stored"), 16)
                    act.wait_ge(sem("k_rope_placed"), 4)

                    def key_std(t):
                        act.wait_ge(sem("k_sums"), t + 1)
                        act.activation(small[:, 3, HEADS * t:HEADS * t + HEADS], small[:, 2, HEADS * t:HEADS * t + HEADS], ACT.Sqrt,
                                       scale=1.0 / QK, bias=eps[:, 0:1]).then_inc(sem("k_stds"), 1)

                    for t in range(NT + 1):
                        for b in range(2):
                            is_filled(act, ("kv", t, b))
                            src = psum(("kv", t, b)).rearrange("p (h e) -> p h e", h=4)
                            act.activation(k_e[:, t, 4 * b:4 * b + 4, 0:NOPE], src[:, :, 0:NOPE], ACT.Copy)
                            done(act.activation(v_e[:, t, 256 * b:256 * b + 256].rearrange("p (h e) -> p h e", h=4),
                                                src[:, :, NOPE:], ACT.Copy))
                        act.wait_ge(sem("read_by_scalar"), groups.count[groups.at[("kv", t, 1)]])
                        n = HEADS * QK
                        act.activation(scratch[:, n * t:n * t + n], k_e[:, t, :, :].rearrange("p h e -> p (h e)"), ACT.Square).then_inc(sem("k_squares"), 1)
                        if t:
                            key_std(t - 1)
                    key_std(NT)
                else:
                    for b in range(12):
                        for t in range(NT):
                            if (b * NT + t) % 2 == 0:
                                is_filled(act, ("qkv", b, t))
                                dst = (q_o, k_o, v_o)[b // 4]
                                done(act.activation(dst[:, t, 256 * (b % 4):256 * (b % 4) + 256], psum(("qkv", b, t))[:, 0:256], ACT.Copy))
                        if b in (4, 8):
                            is_read(act, ("qkv", b - 1, 2))
                            is_read(act, ("qkv", b - 1, 1))
                            buf = (q_o if b == 4 else k_o[:, 0:NT, :]).rearrange("p t n -> p (t n)")
                            head_std(l, b // 4, buf, NT * 2 * HEADS, DK)
                for h in range(HEADS):
                    is_filled(act, ("qT", l, h))
                    n = QK if l == 0 else P
                    done(act.activation(qT[0:n, h, :], psum(("qT", l, h))[0:n, 0:TOK], ACT.Copy))
                units = attention_units(l)
                first = (0, len(attention_units(0)))[l]
                heads_done = output_heads()
                for scores, turned, outs, sums, columns, conv in attention_steps(l):
                    for u in scores:
                        n = P if units[u][1] == 0 else 3 * P
                        act.wait_ge(sem("negmax_ready"), first + u + 1)
                        if u >= 4:
                            is_filled(act, ("pT", l, u - 4))
                        done(act.activation(pbuf[:, u % 4, 0:n], psum(("S", l, u))[:, 0:n], ACT.Exp, bias=negmax[:, u:u + 1],
                                            accum_out=rowsum[:, u:u + 1]))
                    for u in turned:
                        if TURNED_READERS[l][u % 3] == "v":
                            continue
                        n = 1 if units[u][1] == 0 else 3
                        is_filled(act, ("pT", l, u))
                        if u >= 4:
                            is_filled(act, ("o", l, u - 4))
                        done(act.activation(pTbuf[:, u % 4, 0:n, :].rearrange("p a b -> p (a b)"), psum(("pT", l, u))[:, 0:n * P], ACT.Copy))
                    if sums:
                        ada_copy(*sums)
                    if "squares" in conv:
                        is_read(act, "conv_mean")
                        for j in range(NCH):
                            act.activation(conv_sq[:, j, :], conv_acc[:, j, :], ACT.Square).then_inc(sem("conv_squares"), 1)
                    if "std" in conv:
                        is_filled(act, "conv_var")
                        done(act.activation(std[:, :], psum("conv_var")[:, 0:CONVO], ACT.Sqrt, scale=1.0 / CH, bias=eps[:, 0:1]))
                    if l == 1:
                        output_squares(next(heads_done))
                if l == 1:
                    for h in heads_done:
                        output_squares(h)
                    act.wait_ge(sem("scalar_step"), step[0])
                    act.activation(small[:, 1, 0:NT * HEADS], small[:, 0, 0:NT * HEADS], ACT.Sqrt, bias=eps[:, 0:1]).then_inc(sem("output_stds"), 1)
                for j in range((NCH, KD)[l]):
                    is_filled(act, ("oT", l, j))
                    dst, src = hT[:, (NCH, 0)[l] + j, :], psum(("oT", l, j))[:, 0:TOK]
                    done(act.activation(dst, src, ACT.Copy) if l == 0 else act.activation(dst, src, ACT.Identity, scale=col(C_SUB)))
                if l == 0:
                    for j in range(NCH):
                        act.wait_ge(sem("conv_normed"), j + 1)
                        for a, b, src in ((0, CTX, 0), (CTX, TOK, CTX + PADC)):
                            act.activation(hT[:, j, a:b], conv_acc[:, j, src:src + b - a], ACT.Silu, scale=col(C_LNG + j),
                                           bias=col(C_LNB + j)).then_inc(sem("conv_out"), 1)
                squares(l, 1)
                modulated(l, 1)
                for t in range(NT):
                    for b in range(2):
                        is_filled(act, ("htok", l, t, b))
                        done(act.activation(htok[:, t, 512 * b:512 * b + 512], psum(("htok", l, t, b)), ACT.Copy))
                for i, (src, dst, n) in enumerate(((gsub, gexp, NT * NG), (rs[:, R_D, :], rs[:, R_ED, :], NT))):
                    act.wait_ge(sem("exp_asked"), 2 * l + i + 1)
                    act.activation(dst, src, ACT.Exp).then_inc(sem("exp_given"), 1)
                for i in range(NT):
                    is_filled(act, ("codes", l, i))
                    done(act.activation(pair_rows[:, 512 * i:512 * i + 512], psum(("codes", l, i)), ACT.Copy))
                experts(l)
            act.wait_ge(sem("cache_stored"), 64)
            for b in range(2):
                for t in range(NT):
                    if FINAL_READERS[b][t] == "s":
                        is_filled(act, ("final", t, b))
                        done(act.activation(xout[:, t, 512 * b:512 * b + 512], psum(("final", t, b)), ACT.Copy))

        @block.vector
        def _(ve):
            step = [0]

            def mark(ins):
                step[0] += 1
                ins.then_inc(sem("vector_step"), 1)
                return step[0]

            def link(ins):
                ve.wait_ge(sem("vector_step"), mark(ins))

            def done(ins):
                ins.then_inc(sem("read_by_vector"), 1)

            def over(ap, n):
                return ap.unsqueeze(len(ap.shape)).to_broadcast(tuple(ap.shape) + (n,))

            def scaled(out, a, b, op=ALU.mult):
                return ve.tensor_tensor(out=out, in0=a, in1=b, op=op)

            def ada_columns(l, s):
                is_filled(ve, ("adaT", l, s))
                b = cols[:, C_ADA + 48 * l + KD * s:C_ADA + 48 * l + KD * s + KD]
                done(scaled(mod[:, l, s, :, :], psum(("adaT", l, s))[:, 0:2 * KD].rearrange("p (n j) -> p n j", j=2),
                            over(b, 2), ALU.add))
                if s % 3 == 1:
                    is_read(ve, ("adaT", l, s))
                    a = (C_N1 if s == 1 else C_N2) + KD * l
                    ve.scalar_tensor_tensor(out=mod[:, l, s, :, :], in0=mod[:, l, s, :, :], scalar=1.0,
                                            in1=over(cols[:, a:a + KD], 2), op0=ALU.add, op1=ALU.mult).then_inc(sem("scales_ready"), 1)

            def normed(l, w):
                is_read(ve, ("sumsq", l, w))
                link(ve.reciprocal(rstd[:, 0:TOK], std[:, 0:TOK]))
                for c in range(KD):
                    scaled(hn[:, c, :], xT[:, c, :], rstd[:, 0:TOK]).then_inc(sem("hn_ready"), 1)

            def conv_taps():
                for pair in ((0, 1), (2, 3)):
                    before = [0, 0]
                    for k in range(TAPS):
                        for i, j in enumerate(pair):
                            src = uT[:, j, k:k + CONVO]
                            w = col(C_CW + NCH * k + j)
                            if k == 0:
                                ins = ve.tensor_scalar(conv_acc[:, j, :], src, w, col(C_CB + j), ALU.mult, ALU.add)
                            else:
                                ve.wait_ge(sem("vector_step"), before[i])
                                ins = ve.scalar_tensor_tensor(out=conv_acc[:, j, :], in0=src, scalar=w, in1=conv_acc[:, j, :],
                                                              op0=ALU.mult, op1=ALU.add)
                            before[i] = mark(ins)
                        yield k

            def head_norm(i, buf, rows, width, gain, ready):
                k = 2 * (i % 4)
                ve.wait_ge(sem("head_squares"), i + 1)
                ve.tensor_reduce(out=small[:, k, 0:rows], in_=scratch[:, 0:rows * width].rearrange("p (r e) -> p r e", e=width),
                                 axis=AX.X, op=ALU.add).then_inc(sem("head_sums"), 1)
                ve.wait_ge(sem("head_stds"), i + 1)
                link(ve.reciprocal(small[:, k + 1, 0:rows], small[:, k + 1, 0:rows]))
                link(scaled(buf, buf, over(small[:, k + 1, 0:rows], width)))
                scaled(buf, buf, gain.unsqueeze(1).to_broadcast((P, rows, width))).then_inc(sem(ready), 1)

            def mixer_residual(l):
                for c in range(KD):
                    is_filled(ve, ("out", l, c))
                    for a, b, j in SEG:
                        ins = ve.scalar_tensor_tensor(out=xT[:, c, a:b], in0=psum(("out", l, c))[:, a:b], scalar=mcol(l, 2, c, j),
                                                      in1=xT[:, c, a:b], op0=ALU.mult, op1=ALU.add)
                    done(ins)

            def expert_residual(l, r, pair):
                for k in range(2):
                    c = 2 * r + k
                    for a, b, j in SEG:
                        ins = ve.scalar_tensor_tensor(out=xT[:, c, a:b], in0=bank[pair + k][:, a:b], scalar=mcol(l, 5, c, j),
                                                      in1=xT[:, c, a:b], op0=ALU.mult, op1=ALU.add)
                return ins

            def attention(l, taps):
                units = attention_units(l)
                for scores, turned, outs, sums, columns, conv in attention_steps(l):
                    for u in scores:
                        n = P if units[u][1] == 0 else 3 * P
                        is_filled(ve, ("S", l, u))
                        ve.tensor_reduce(out=negmax[:, u:u + 1], in_=psum(("S", l, u))[:, 0:n], axis=AX.X, op=ALU.max,
                                         negate=True).then_inc(sem("negmax_ready"), 1)
                    next(taps, None)
                    for u in turned:
                        if TURNED_READERS[l][u % 3] == "v":
                            n = 1 if units[u][1] == 0 else 3
                            is_filled(ve, ("pT", l, u))
                            if u >= 4:
                                is_filled(ve, ("o", l, u - 4))
                            done(ve.tensor_copy(pTbuf[:, u % 4, 0:n, :].rearrange("p a b -> p (a b)"), psum(("pT", l, u))[:, 0:n * P]))
                    for u in outs:
                        h, t, m = units[u]
                        is_read(ve, ("S", l, u))
                        link(ve.reciprocal(rinv[:, u:u + 1], rowsum[:, u:u + 1]))
                        if m == 0:
                            w = NOPE if l == 0 else DV
                            dst = (o_e if l == 0 else o_o)[:, t, w * h:w * h + w]
                            is_filled(ve, ("o", l, u))
                            done(ve.tensor_scalar(dst, psum(("o", l, u))[:, 0:w], rinv[:, u:u + 1], None, ALU.mult))
                        else:
                            link(scaled(rinv[:, u:u + 1], rinv[:, u:u + 1], lam[:, 5:6]))
                            dst = o_o[:, t, DV * h:DV * h + DV]
                            is_filled(ve, ("o", l, u))
                            is_read(ve, ("o", l, u - 1))
                            done(ve.scalar_tensor_tensor(out=dst, in0=psum(("o", l, u))[:, 0:DV], scalar=rinv[:, u:u + 1],
                                                         in1=dst, op0=ALU.mult, op1=ALU.add))
                    if columns:
                        ada_columns(*columns)
                    if "mean" in conv:
                        assert next(taps, None) is None
                        ve.wait_ge(sem("vector_step"), step[0])
                        ve.nop().then_inc(sem("conv_ready"), 1)
                    if "centre" in conv:
                        is_filled(ve, "conv_mean")
                        for j in range(NCH):
                            ins = ve.scalar_tensor_tensor(out=conv_acc[:, j, :], in0=psum("conv_mean")[:, 0:CONVO], scalar=-1.0 / CH,
                                                          in1=conv_acc[:, j, :], op0=ALU.mult, op1=ALU.add)
                        done(ins)
                    if "normed" in conv:
                        is_read(ve, "conv_var")
                        link(ve.reciprocal(rstd[:, :], std[:, :]))
                        for j in range(NCH):
                            scaled(conv_acc[:, j, :], conv_acc[:, j, :], rstd[:, :]).then_inc(sem("conv_normed"), 1)
                if l == 1:
                    ve.wait_ge(sem("output_stds"), 1)
                    r = small[:, 1, 0:NT * HEADS]
                    link(ve.reciprocal(r, r))
                    for h in range(HEADS):
                        x = o_o[:, :, DV * h:DV * h + DV]
                        scaled(x, x, over(r[:, NT * h:NT * h + NT], DV)).then_inc(sem("o_normed"), 1)
                for _ in taps:
                    pass

            def routing(l):
                k = B_MOE + (NG + NE) * l
                is_filled(ve, ("router", l))
                done(scaled(logits[:, :, :], psum(("router", l))[:, 0:NT * (NG + NE)].rearrange("p (t e) -> p t e", t=NT),
                            bc[:, k:k + NG + NE].unsqueeze(1).to_broadcast((P, NT, NG + NE)), ALU.add))
                is_read(ve, ("router", l))

                def m(i):
                    return rt[:, i, :].rearrange("p (t e) -> p t e", t=NT)

                def g(ap):
                    return ap.rearrange("p (t e) -> p t e", t=NT)

                def r(i):
                    return rs[:, i, :]

                def top(out, src, op=ALU.max):
                    link(ve.tensor_reduce(out=out, in_=src, axis=AX.X, op=op))

                def first_of_equals(one, src, value, eq, rank, best, n):
                    link(scaled(eq, src, over(r(value), n), ALU.is_equal))
                    link(scaled(rank, eq, ramp[:, NE - n:NE].unsqueeze(1).to_broadcast((P, NT, n))))
                    top(r(best), rank)
                    link(scaled(one, rank, over(r(best), n), ALU.is_equal))

                gl, el = logits[:, :, 0:NG], logits[:, :, NG:]
                top(r(R_GMAX), gl)
                scaled(g(gsub), gl, over(r(R_GMAX), NG), ALU.subtract).then_inc(sem("exp_asked"), 1)
                first_of_equals(g(gone), gl, R_GMAX, g(geq), g(grank), R_GTOP, NG)
                link(ve.tensor_scalar(g(gpen), g(gone), BIG, -BIG, ALU.mult, ALU.add))
                link(scaled(rt[:, M_SEL, :].rearrange("p (t g e) -> p t g e", t=NT, g=NG),
                            el.rearrange("p t (g e) -> p t g e", g=NG), over(g(gpen), EPG), ALU.add))
                top(r(R_M1), m(M_SEL))
                first_of_equals(m(M_ONE1), m(M_SEL), R_M1, m(M_EQ), m(M_WORK), R_TOP1, NE)
                link(ve.scalar_tensor_tensor(out=m(M_SEL2), in0=m(M_ONE1), scalar=-BIG, in1=m(M_SEL), op0=ALU.mult, op1=ALU.add))
                top(r(R_M2), m(M_SEL2))
                scaled(r(R_D), r(R_M2), r(R_M1), ALU.subtract).then_inc(sem("exp_asked"), 1)
                first_of_equals(m(M_ONE2), m(M_SEL2), R_M2, m(M_EQ), m(M_WORK), R_TOP2, NE)
                scaled(m(M_BOTH), m(M_ONE1), m(M_ONE2), ALU.add).then_inc(sem("chosen"), 1)
                ve.wait_ge(sem("exp_given"), 2 * l + 2)
                top(r(R_GSUM), g(gexp), ALU.add)
                link(ve.tensor_scalar(r(R_D), r(R_ED), 1.0, None, ALU.add))
                link(scaled(r(R_GATE), r(R_GSUM), r(R_D)))
                link(ve.reciprocal(r(R_W1), r(R_GATE)))
                link(scaled(r(R_W2), r(R_W1), r(R_ED)))
                is_filled(ve, ("rank", l))
                pr = psum(("rank", l))
                count = pr[:, NE * NT:NE * NT + NE]
                link(ve.tensor_copy(prefix[:, 0, 16:], count))
                a = 0
                for d in (1, 2, 4, 8, 16):
                    link(scaled(prefix[:, 1 - a, 16:], prefix[:, a, 16:], prefix[:, a, 16 - d:16 - d + NE], ALU.add))
                    a = 1 - a
                link(scaled(prefix[:, a, 16:], prefix[:, a, 16:], pr[:, NE * NT:NE * NT + NE], ALU.subtract))
                link(ve.tensor_copy(rt[:, M_RANK, :], pr[:, 0:NE * NT]))
                link(scaled(m(M_PLACE), m(M_RANK), prefix[:, a, 16:].unsqueeze(1).to_broadcast((P, NT, NE)), ALU.add))

                def both(i):
                    return rt[:, i:i + 2, :].rearrange("p k (t e) -> p k t e", t=NT)

                def of_the_choices(w, into):
                    link(scaled(both(M_WORK), both(M_ONE1), w.unsqueeze(1).to_broadcast((P, 2, NT, NE))))
                    top(rs[:, into:into + 2, :], both(M_WORK), ALU.add)

                of_the_choices(m(M_PLACE), R_P1)
                ins = ve.tensor_copy(idx_sorted[:, :], rs[:, R_P1:R_P2 + 1, :].rearrange("p k t -> p (k t)"))
                ins.then_inc(sem("places_ready"), 1)
                ve.wait_ge(sem("places_ready"), l + 1)
                if l:
                    ve.wait_ge(sem("rowsT_ready"), NE)
                first = rt[:, M_SEL:M_SEL2 + 1, :].rearrange("p a (j e) -> p (a j) e", e=NE)
                link(scaled(first, prefix[:, a, 16:].unsqueeze(1).to_broadcast((P, ROUNDS, NE)), over(turn_row[:, 0:ROUNDS], NE), ALU.add))
                link(ve.tensor_scalar(starts[:, :].rearrange("p (j e) -> p j e", e=NE), first, float(PAIRS), None, ALU.min))
                link(ve.tensor_reduce(out=rs[:, R_TURN, 0:1], in_=count, axis=AX.X, op=ALU.max))
                link(ve.tensor_scalar(overflow[:, l:l + 1], rs[:, R_TURN, 0:1], float(ROWS), None, ALU.is_gt))
                ve.nop().then_inc(sem("starts_ready"), 1)
                done(ve.nop())
                of_the_choices(m(M_RANK), R_RANK1)
                of_the_choices(turn_row[:, :].unsqueeze(1).to_broadcast((P, NT, NE)), R_ID1)
                ids = rs[:, R_ID1:R_ID2 + 1, :].rearrange("p k t -> p (k t)")
                ranks = rs[:, R_RANK1:R_RANK2 + 1, :].rearrange("p k t -> p (k t)")
                late = rt[:, M_WORK, 0:2 * NT * (ROUNDS - 1)].rearrange("p (i j) -> p i j", j=ROUNDS - 1)
                link(scaled(late, over(ranks, ROUNDS - 1), turn_row[:, 1:ROUNDS].unsqueeze(1).to_broadcast((P, 2 * NT, ROUNDS - 1)), ALU.is_ge))
                places = rs[:, R_P1:R_P2 + 1, :].rearrange("p k t -> p (k t)")
                top(places, late, ALU.add)
                link(scaled(ids, ids, ranks, ALU.add))
                link(ve.scalar_tensor_tensor(out=ids, in0=places, scalar=float(NE * ROWS - ROWS), in1=ids, op0=ALU.mult, op1=ALU.add))
                scaled(diagonals, ident[:, :].unsqueeze(1).to_broadcast((P, 4 * NT, P)),
                       over(rs[:, R_ID1:R_ID1 + 4, :].rearrange("p k t -> p (k t)"), P)).then_inc(sem("diagonals_ready"), 1)
                ve.tensor_scalar(pair_codes, turn_row[:, 0:NE:2], row_of[:, 0:1], None, ALU.add).then_inc(sem("pair_codes_ready"), 1)

            def experts(l):
                base = NE * l

                def hidden(n, t=0):
                    ve.wait_ge(sem("silu_done"), UNROLL * t + (base + n + 1))
                    up = psum(("first", l)) if n == 0 else bank[1]
                    scaled(hid[:, n % BUFFERS, :], sgate[:, n % BUFFERS, :], up[ROWS:2 * ROWS, 0:FF]).then_inc(sem("hid_ready"), 1)

                def place_weights(q, t=0):
                    count = UNROLL // 2 * t + (NE // 2 * l + q)
                    if NE // 2 * l + q:
                        ve.wait_ge(sem("weights_placed"), count)
                    place(weights_at[q % BUFFERS], pair_codes[:, bass.ds(UNROLL // 2 * t + q, 1)],
                          sem("choices_placed"), count + 1, sem("weights_placed"))

                def place(out, code, half_way, count, ready):
                    ve.scalar_tensor_tensor(out=chosen_by, in0=pair_rows[:, 0:2 * TOK], scalar=code, in1=pair_rows[:, 2 * TOK:4 * TOK],
                                            op0=ALU.is_equal, op1=ALU.mult).then_inc(half_way, 1)
                    ve.wait_ge(half_way, count)
                    scaled(out, chosen_by[:, 0:TOK], chosen_by[:, TOK:2 * TOK], ALU.add).then_inc(ready, 1)

                def add(q, rounds, t=0):
                    for r in rounds:
                        ve.wait_ge(sem("spread_filled"), PAIR_ROUNDS * (UNROLL // 2) * t + (PAIR_ROUNDS * (NE // 2 * l + q) + r + 1))
                        expert_residual(l, r, 4 + 2 * (r % 2)).then_inc(sem("spread_added"), 1)

                def step(n, t=0):
                    hidden(n, t)
                    if n % 2 == 0:
                        place_weights(n // 2 - 1, t)
                    if n >= 3:
                        add((n - 3) // 2, ((0, 1), (2, 3))[(n - 3) % 2], t)

                ve.wait_ge(sem("cache_stored"), 32 * (l + 1))
                for i in range(PAIRS // P):
                    is_filled(ve, ("sorted", l, i, 0))
                    done(ve.tensor_copy(sortedT[:, 0:4, P * i:P * i + P], psum(("sorted", l, i, 0)).rearrange("p (c r) -> p c r", c=4)))
                hidden(0)
                ve.wait_ge(sem("hid_ready"), base + 1)
                done(ve.nop())
                is_read(ve, ("codes", l, NT - 1))
                ve.wait_ge(sem("pair_codes_ready"), l + 1)
                for n in range(1, STEPS_AHEAD + 1):
                    step(n)
                with ve.Fori(0, BODIES) as t:
                    for n in range(STEPS_AHEAD + 1, STEPS_AHEAD + 1 + UNROLL):
                        step(n, t)
                for n in range(STEPS_AHEAD + 1 + UNROLL * BODIES, NE):
                    step(n)
                place_weights(NE // 2 - 1)
                add(NE // 2 - 2, (2, 3))
                add(NE // 2 - 1, (0, 1, 2, 3))

                def further_turn(i):
                    ve.wait_ge(sem(f"further{l}_rows_turned"), i + 1)
                    ve.tensor_copy(teT[0].rearrange("p c r -> p (c r)"), bank[0][:, :]).then_inc(sem(f"further{l}_rowsT"), 1)
                    ve.tensor_scalar(further_code[:, :], further_code[:, :], float(ROWS), None, ALU.add).then_inc(sem(f"further{l}_code"), 1)
                    ve.wait_ge(sem(f"further{l}_code"), i + 2)
                    place(weights_at[0], further_code[:, 0:1], sem(f"further{l}_choices"), i + 1, sem(f"further{l}_weights"))
                    ve.wait_ge(sem(f"further{l}_weights"), i + 1)
                    ve.wait_ge(sem(f"further{l}_silu"), i + 1)
                    scaled(hid[:, 0, :], sgate[:, 0, :], bank[2][0:ROWS, 0:FF]).then_inc(sem(f"further{l}_hid"), 1)
                    ve.wait_ge(sem(f"further{l}_down"), i + 1)
                    ve.tensor_copy(y_further[:, 0:512], bank[4][0:ROWS, :])
                    ve.tensor_copy(y_further[:, 512:D], bank[5][0:ROWS, :]).then_inc(sem(f"further{l}_y"), 1)
                    for r in range(PAIR_ROUNDS):
                        ve.wait_ge(sem(f"further{l}_spread"), PAIR_ROUNDS * i + (r + 1))
                        expert_residual(l, r, 6).then_inc(sem(f"further{l}_added"), 1)
                    ve.wait_ge(sem(f"further{l}_added"), PAIR_ROUNDS * i + PAIR_ROUNDS)

                many = ve.value_load(overflow[0:1, l:l + 1], min_val=0, max_val=1)
                with ve.If(many > 0):
                    ve.wait_ge(sem("spread_added"), PAIR_ROUNDS * NE // 2 * (l + 1))
                    ve.tensor_scalar(further_code[:, :], row_of[:, :], float(NE * ROWS - ROWS), None, ALU.add).then_inc(sem(f"further{l}_code"), 1)
                    ve.wait_ge(sem(f"further{l}_code"), 1)
                    with ve.Fori(0, (ROUNDS - 1) * NE) as i:
                        further_turn(i)

            ve.memset(eps[:, :], EPS)
            ve.memset(prefix[:, :, :], 0.0)
            ve.memset(condS[:, :, :], 0.0)
            ve.memset(uT, 0.0).then_inc(sem("constants_ready_v"), 1)
            ve.wait_ge(sem("constants_ready_v"), 1)
            is_filled(ve, "vectors")
            done(ve.tensor_copy(cols[:, :], psum("vectors")[:, 0:NCOL]))
            is_read(ve, "vectors")
            ve.wait_ge(sem("constants_ready"), 1)
            link(ve.tensor_copy(turn_row[:, :], iota[:, :]))
            link(ve.tensor_copy(row_of[:, :], row_iota[:, :]))
            link(ve.tensor_scalar(ramp[:, :], turn_row[:, :], -1.0 / ROWS, float(NE), ALU.mult, ALU.add))
            normed(0, 0)
            for s in range(2):
                ada_columns(0, s)
            for l in range(DEPTH):
                if l:
                    normed(l, 0)
                taps = iter(())
                if l == 0:
                    ve.wait_ge(sem("rows_of_gains_loaded"), 16 * 13)
                    link(ve.tensor_scalar(col(C_SUB), col(C_SUB), 1.0 - LAMBDA_INIT, None, ALU.mult))
                    for a, n, f in ((B_QN, QK, QK ** -0.5), (B_DQN, DK, DK ** -0.5)):
                        link(ve.tensor_scalar(bc[:, a:a + n], bc[:, a:a + n], f, None, ALU.mult))
                    for i in range(2):
                        a = B_LAM + 2 * DK * i
                        link(scaled(bc[:, a:a + DK], bc[:, a:a + DK], bc[:, a + DK:a + 2 * DK]))
                        ins = ve.tensor_reduce(out=lam[:, i:i + 1], in_=bc[:, a:a + DK], axis=AX.X, op=ALU.add)
                        if i == 0:
                            link(ins)
                        else:
                            ins.then_inc(sem("lambda_sums"), 1)
                    taps = conv_taps()
                    for i, (kind, js) in enumerate(IN_BLOCKS):
                        if kind == "glu_g":
                            for j in js:
                                is_read(ve, ("glu_g", j))
                                for a, b, dst in ((0, CTX, PADC), (CTX, TOK, 2 * PADC + CTX)):
                                    ins = scaled(uT[:, j, dst:dst + b - a], glu_a[:, j, a:b], glu_g[:, j, a:b])
                                    ins.then_inc(sem("u_ready"), 1)
                            ve.wait_ge(sem("u_ready"), 2 * js[1] + 2)
                        if i - 1 in ADA_AFTER_BLOCK:
                            ada_columns(*ADA_AFTER_BLOCK[i - 1])
                        for _ in range((0, 15, 16, 10, 10, 5, 0)[i]):
                            next(taps)
                    ve.wait_ge(sem("lambda_exps"), 1)
                    link(scaled(lam[:, 4:5], lam[:, 3:4], lam[:, 2:3], ALU.subtract))
                    link(ve.tensor_scalar(lam[:, 5:6], lam[:, 4:5], -LAMBDA_INIT, None, ALU.add))
                    ve.wait_ge(sem("u_ready"), 8)
                    ve.wait_ge(sem("latent_std"), 1)
                    link(ve.reciprocal(small[:, 7, 0:2 * NT], small[:, 7, 0:2 * NT]))
                    for t in range(NT):
                        ve.tensor_scalar(proj[:, t, 0:QR], proj[:, t, 0:QR], small[:, 7, 2 * t:2 * t + 1], None,
                                         ALU.mult).then_inc(sem("qa_normed"), 1)
                    for t in range(NT):
                        ve.scalar_tensor_tensor(out=ckv[:, t, :], in0=proj[:, t, QR:QR + KVR], scalar=small[:, 7, 2 * t + 1:2 * t + 2],
                                                in1=bc[:, B_KVN:B_KVN + KVR], op0=ALU.mult, op1=ALU.mult).then_inc(sem("ckv_normed"), 1)
                    ve.wait_ge(sem("pad_stored"), 16)
                    ve.wait_ge(sem("cache_loaded"), 32)
                    for t in range(4):
                        src = proj[:, t, QR + KVR:REST] if t < NT else krope_c
                        ve.tensor_copy(k_e[:, t, :, NOPE:], src.unsqueeze(1).to_broadcast((P, HEADS, ROPE))).then_inc(sem("k_rope_placed"), 1)
                    for j in range(2):
                        is_filled(ve, ("ckvT", j))
                        done(ve.tensor_copy(ckvT[:, j, :], psum(("ckvT", j))))
                    for b in range(2):
                        for t in range(NT):
                            is_filled(ve, ("q", b, t))
                            done(ve.tensor_copy(q_e[:, t, 384 * b:384 * b + 384], psum(("q", b, t))[:, 0:384]))
                    is_read(ve, ("q", 1, 2))
                    head_norm(0, a1[:, 0:NT * HEADS * QK].rearrange("p (r e) -> p r e", e=QK), NT * HEADS, QK, bc[:, B_QN:B_QN + QK], "heads_normed")
                    gain = bc[:, B_KN:B_KN + QK].unsqueeze(1).to_broadcast((P, HEADS, QK))

                    def keys_normed(t):
                        ve.wait_ge(sem("k_stds"), t + 1)
                        r, x = small[:, 3, HEADS * t:HEADS * t + HEADS], k_e[:, t, :, :]
                        link(ve.reciprocal(r, r))
                        link(scaled(x, x, over(r, QK)))
                        scaled(x, x, gain).then_inc(sem("k_normed"), 1)

                    for t in range(NT + 1):
                        ve.wait_ge(sem("k_squares"), t + 1)
                        n = HEADS * QK
                        ve.tensor_reduce(out=small[:, 2, HEADS * t:HEADS * t + HEADS], in_=scratch[:, n * t:n * t + n].rearrange("p (r e) -> p r e", e=QK),
                                         axis=AX.X, op=ALU.add).then_inc(sem("k_sums"), 1)
                        if t:
                            keys_normed(t - 1)
                    keys_normed(NT)
                    ve.wait_ge(sem("cache_stored"), 32)
                else:
                    for b in range(12):
                        for t in range(NT):
                            if (b * NT + t) % 2:
                                is_filled(ve, ("qkv", b, t))
                                dst = (q_o, k_o, v_o)[b // 4]
                                done(ve.tensor_copy(dst[:, t, 256 * (b % 4):256 * (b % 4) + 256], psum(("qkv", b, t))[:, 0:256]))
                        if b in (4, 8):
                            buf, gain = ((a1[:, :], B_DQN), (a2[:, 0:3072], B_DKN))[b // 4 - 1]
                            is_read(ve, ("qkv", b - 1, 2))
                            is_read(ve, ("qkv", b - 1, 1))
                            head_norm(b // 4, buf.rearrange("p (r e) -> p r e", e=DK), NT * 2 * HEADS, DK, bc[:, gain:gain + DK], "heads_normed")
                for h in range(HEADS):
                    is_filled(ve, ("kT", l, h))
                    n = QK if l == 0 else P
                    done(ve.tensor_copy(kT[0:n, h, :], psum(("kT", l, h))[0:n, :]))
                attention(l, taps)
                mixer_residual(l)
                normed(l, 1)
                routing(l)
                experts(l)
            ve.wait_ge(sem("cache_stored"), 64)
            for b in range(2):
                for t in range(NT):
                    if FINAL_READERS[b][t] == "v":
                        is_filled(ve, ("final", t, b))
                        done(ve.tensor_copy(xout[:, t, 512 * b:512 * b + 512], psum(("final", t, b))))

        @block.gpsimd
        def _(pool):
            step = [0]

            def link(ins):
                step[0] += 1
                ins.then_inc(sem("pool_step"), 1)
                pool.wait_ge(sem("pool_step"), step[0])

            def rope(x1, x2, cos, sin, tmp, ready, count=0):
                a, b, c = tmp
                tt = pool.tensor_tensor
                tt(out=a, in0=x1, in1=sin, op=ALU.mult)
                tt(out=b, in0=x2, in1=cos, op=ALU.mult)
                link(tt(out=c, in0=x2, in1=sin, op=ALU.mult))
                link(tt(out=x1, in0=x1, in1=cos, op=ALU.mult))
                link(tt(out=x1, in0=x1, in1=c, op=ALU.subtract))
                ins = tt(out=x2, in0=a, in1=b, op=ALU.add)
                if ready:
                    ins.then_inc(sem(ready), 1)
                    pool.wait_ge(sem(ready), count)
                else:
                    link(ins)

            link(pool.memset(ident[:, :], 0.0))
            link(pool.memset(ones[:, :], 1.0))
            link(pool.affine_select(out=ident[:, :], in_=ident[:, :], compare_op=ALU.not_equal, fill=1.0, base=0,
                                    pattern=[[-1, P]], channel_multiplier=1))
            link(pool.affine_select(out=below[:, :], in_=ones[:, :], compare_op=ALU.is_gt, fill=0.0, base=0,
                                    pattern=[[1, P]], channel_multiplier=-1))
            link(pool.memset(pick[:, :, :], 0.0))
            for beyond in (0, 64):
                link(pool.affine_select(out=pick[:, :, :], in_=pick[:, :, :], compare_op=ALU.not_equal, fill=1.0, base=-beyond,
                                        pattern=[[-32, 2], [-1, 2]], channel_multiplier=1))
            link(pool.iota(row_iota[:, :], pattern=[[1, 1]], base=0, channel_multiplier=1))
            pool.iota(iota[:, :], pattern=[[ROWS, NE]], base=0, channel_multiplier=0).then_inc(sem("constants_ready"), 1)
            link(pool.memset(a7[0:ROWS, 0:D], 0.0))
            pool.dma_start(sorted_rows[PAIRS:PAIRS + ROWS, :], a7[0:ROWS, 0:D]).then_inc(sem("pad_stored"), 16)
            pool.wait_ge(sem("pad_stored"), 16)
            for v, k in ((qn_g[0], B_QN), (kn_g[0], B_KN), (dqn_g[0], B_DQN), (dkn_g[0], B_DKN),
                         (kvn_g[0], B_KVN), (lq1[0], B_LAM), (lk1[0], B_LAM + DK), (lq2[0], B_LAM + 2 * DK),
                         (lk2[0], B_LAM + 3 * DK), (moe_bg[0], B_MOE), (moe_be[0], B_MOE + NG),
                         (moe_bg[1], B_MOE + NG + NE), (moe_be[1], B_MOE + 2 * NG + NE)):
                pool.dma_start(bc[:, k:k + v.shape[0]], v.partition_broadcast(P)).then_inc(sem("rows_of_gains_loaded"), 16)
            pool.dma_start(rope16[:, :, :, :], rope_mla.rearrange("(t p) a n -> p t a n", p=P)).then_inc(sem("rope_loaded"), 16)
            pool.dma_start(rope32[:, :, :, :], rope_diff.rearrange("(t p) a n -> p t a n", p=P)).then_inc(sem("rope_loaded"), 16)
            for l in range(DEPTH):
                pool.dma_start(wr[:, l, :, 0:NG], moe_wg[l].rearrange("(k p) g -> p k g", p=P)).then_inc(sem("router_loaded"), 16)
                pool.dma_start(wr[:, l, :, NG:], moe_we[l].rearrange("(k p) g -> p k g", p=P)).then_inc(sem("router_loaded"), 16)

            def modulated(l, w):
                is_read(pool, ("adaT", l, 3 * w + 1))
                pool.wait_ge(sem("scales_ready"), 2 * l + w + 1)
                for c in range(KD):
                    pool.wait_ge(sem("hn_ready"), KD * (2 * l + w) + c + 1)
                    pool.tensor_scalar(hT[:, c, 0:CTX], hn[:, c, 0:CTX], mcol(l, 3 * w + 1, c, 0), mcol(l, 3 * w, c, 0),
                                       ALU.mult, ALU.add).then_inc(sem("h_ctx_ready"), 1)

            for l in range(DEPTH):
                modulated(l, 0)
                if l == 0:
                    pool.wait_ge(sem("rope_loaded"), 32)
                    is_read(pool, ("rest", 2, 0))
                    pool.wait_ge(sem("ckv_normed"), 1)
                    pool.dma_start(new_ckv[0, 0], ckv[:, 0, :]).then_inc(sem("cache_stored"), 16)
                    pool.dma_start(new_krope[0, 0], proj[:, 0, QR + KVR:REST]).then_inc(sem("cache_stored"), 16)
                    half = ROPE // 2
                    for buf, normed, ready in ((a1, "heads_normed", "q_ready"), (a2, "k_normed", "k_ready")):
                        for t in (1, 2):
                            pool.wait_ge(sem(normed), 1 if buf is a1 else t + 1)
                            x = buf[:, t * HEADS * QK:(t + 1) * HEADS * QK].rearrange("p (h e) -> p h e", h=HEADS)
                            cos, sin = (rope16[:, t - 1, k, :].unsqueeze(1).to_broadcast((P, HEADS, half)) for k in range(2))
                            tmp = [rope_tmp[:, k, 0:HEADS * half].rearrange("p (h e) -> p h e", h=HEADS) for k in range(3)]
                            rope(x[:, :, NOPE:NOPE + half], x[:, :, NOPE + half:], cos, sin, tmp, ready if t == 2 else None, 1)
                else:
                    for i, (buf, ready) in enumerate(((q_o, "q_ready"), (k_o, "k_ready"))):
                        pool.wait_ge(sem("heads_normed"), i + 2)
                        if i == 1:
                            pool.dma_start(new_dk[0, 0].rearrange("p h m d -> p (h m d)"), k_o[:, 0, :]).then_inc(sem("cache_stored"), 16)
                        half = DK // 2
                        for t in (1, 2):
                            x = buf[:, t, :].rearrange("p (r e) -> p r e", e=DK)
                            cos, sin = (rope32[:, t - 1, k, :].unsqueeze(1).to_broadcast((P, 2 * HEADS, half)) for k in range(2))
                            tmp = [rope_tmp[:, k, :].rearrange("p (r e) -> p r e", e=half) for k in range(3)]
                            rope(x[:, :, 0:half], x[:, :, half:], cos, sin, tmp, ready if t == 2 else None, 2)
                    for b in (10, 11):
                        is_read(pool, ("qkv", b, 0))
                    pool.dma_start(new_dv[0, 0].rearrange("p h d -> p (h d)"), v_o[:, 0, :]).then_inc(sem("cache_stored"), 16)
                modulated(l, 1)
                is_read(pool, ("htok", l, NT - 1, 1))
                pool.wait_ge(sem("cache_stored"), 32 * (l + 1))
                link(pool.memset(sortedT[:, :, PAIRS:], 0.0))
                pool.wait_ge(sem("places_ready"), l + 1)
                for k in range(2):
                    for t in range(NT):
                        pool.indirect_dma_start(out=sorted_rows, out_offset=bass.IndirectOffsetOnAxis(ap=idx_sorted[:, NT * k + t:NT * k + t + 1], axis=0),
                                                in_=htok[:, t, :], in_offset=None).then_inc(sem("rows_sorted"), 16)
                pool.wait_ge(sem("starts_ready"), l + 1)
                is_read(pool, ("sorted", l, PAIRS // P - 1, 0))
                is_read(pool, ("sorted", l, PAIRS // P - 1, 1))

                def rows_copy(n, t=0):
                    if NE * l + n >= BUFFERS:
                        pool.wait_ge(sem("gate_up_filled"), BUFFERS * t + (NE * l + n - 1))
                    first = pool.value_load(starts[0:1, bass.ds(BUFFERS * t + n, 1)], min_val=0, max_val=PAIRS)
                    pool.tensor_copy(teT[n % BUFFERS], sortedT[:, :, bass.ds(first, ROWS)]).then_inc(sem("rowsT_ready"), 1)

                pool.nop().then_inc(sem("rowsT_ready"), 1)
                rows_copy(1)
                with pool.Fori(0, NE // BUFFERS - 1) as t:
                    for n in range(BUFFERS, 2 * BUFFERS):
                        rows_copy(n, t)
            pool.wait_ge(sem("cache_stored"), 64)


def rope_tables(rot):
    quarter = rot // 4
    freqs = np.power(np.float32(10000.0), -np.arange(quarter, dtype=np.float32) / np.float32(quarter)).astype(np.float32)
    row = np.repeat(np.arange(LAT // 64, dtype=np.float32), 64)
    column = np.tile(np.arange(64, dtype=np.float32), LAT // 64)
    angle = np.concatenate([row[:, None] * freqs, column[:, None] * freqs], axis=-1)
    return np.stack([np.cos(angle), np.sin(angle)], axis=1).astype(np.float32)


_OUTS = [((1, 128, 1024), "float32"), ((1, 256, 1024), "float32"), ((1, 1, 128, 256), "float32"),
         ((1, 1, 128, 32), "float32"), ((1, 1, 128, 8, 2, 64), "float32"), ((1, 1, 128, 8, 128), "float32")]


def kernel(**inputs):
    import numpy as _np
    import concourse.bacc as _bacc
    from concourse import mybir as _mybir
    from concourse.bass_utils import run_bass_kernel_spmd as _run

    nc = _bacc.Bacc("TRN2", target_bir_lowering=False, num_devices=1)
    arrays, args = {}, []
    material = {name: inputs[name] for name in MATERIAL}
    material["rope_mla"], material["rope_diff"] = rope_tables(ROPE), rope_tables(DK)
    for name, a in material.items():
        a = _np.ascontiguousarray(a)
        arrays[f"in_{name}_dram"] = a
        args.append(nc.dram_tensor(f"in_{name}_dram", a.shape, _mybir.dt.from_np(a.dtype), kind="ExternalInput").ap())
    outs = [nc.dram_tensor(f"out_{i}_dram", shape, _mybir.dt.from_np(_np.dtype(dtype)), kind="ExternalOutput").ap()
            for i, (shape, dtype) in enumerate(_OUTS)]
    hybrid_trunk(nc, args[:-2], args[-2:], outs)
    r = _run(nc, [arrays], core_ids=[0])
    return tuple(r.results[0][f"out_{i}_dram"] for i in range(len(_OUTS)))
```
